# Optimizing a Trainium2 kernel written in Bass

```python
import jax, jax.numpy as jnp
from jax import lax
import numpy as np

D_MODEL = 1024
BATCH = 1
SEQ = 512
DEPTH = 1
DEC_BATCH = 1
DEC_SEQ = 32
PAST_LEN = 256

CHUNK = 64
D_CONV = D_MODEL // 2
CONV_A_W = 3
D_SSD = D_MODEL // 2
SSD_HEAD_DIM = 64
SSD_HEADS = D_SSD // SSD_HEAD_DIM
SSD_GROUPS = 2
SSD_HPG = SSD_HEADS // SSD_GROUPS
SSD_STATE = 128
SSD_CONV_W = 4
XBC_DIM = D_SSD + 2 * SSD_GROUPS * SSD_STATE
IN_SIZES = (D_CONV, D_CONV, D_CONV, D_SSD, XBC_DIM, SSD_HEADS)
IN_DIM = sum(IN_SIZES)
D_MIX = D_CONV + D_SSD
N_MEM = 256
MEM_HEADS = 4
MEM_HEAD_DIM = D_MODEL // MEM_HEADS
D_ATT = MEM_HEADS * MEM_HEAD_DIM
PEER_HEADS = 8
N_KEYS = 128
N_EXPERTS = N_KEYS * N_KEYS
PEER_TOPK = 16
PEER_DK = 256
PEER_DK_HALF = PEER_DK // 2
PEER_BLOCK = 128
EPS = 1e-6

kernel_name = "hybrid_stream_conv_ssd_peer_step"

def rmsnorm(x, g):
    xf = x.astype(jnp.float32)
    y = xf * lax.rsqrt(jnp.mean(xf * xf, axis=-1, keepdims=True) + EPS)
    return (y * g.astype(jnp.float32)).astype(x.dtype)

def causal_dwconv(u, hist, w):
    cat = jnp.concatenate([hist.astype(u.dtype), u], axis=1)
    y = lax.conv_general_dilated(cat, w[:, None, :].astype(u.dtype), window_strides=(1,),
                                 padding='VALID', dimension_numbers=('NWC', 'WIO', 'NWC'),
                                 feature_group_count=u.shape[-1])
    return y, cat[:, -(w.shape[0] - 1):]

def ssd_scan(x, dt, A, Bm, Cm, h0):
    b, s = x.shape[:2]
    l = min(CHUNK, s)
    c = s // l
    f32 = jnp.float32
    xr = x.astype(f32).reshape(b, c, l, SSD_GROUPS, SSD_HPG, SSD_HEAD_DIM)
    dtr = dt.reshape(b, c, l, SSD_GROUPS, SSD_HPG)
    Br = Bm.astype(f32).reshape(b, c, l, SSD_GROUPS, SSD_STATE)
    Cr = Cm.astype(f32).reshape(b, c, l, SSD_GROUPS, SSD_STATE)
    acum = jnp.cumsum(dtr * A.astype(f32).reshape(SSD_GROUPS, SSD_HPG), axis=2)
    seg = acum[:, :, :, None] - acum[:, :, None, :]
    mask = jnp.tril(jnp.ones((l, l), bool))[:, :, None, None]
    Lm = jnp.exp(jnp.where(mask, seg, -jnp.inf))
    xdt = xr * dtr[..., None]
    CB = jnp.einsum('bclgn,bcsgn->bclsg', Cr, Br)
    y_diag = jnp.einsum('bclsg,bclsgh,bcsghp->bclghp', CB, Lm, xdt)
    decay = jnp.exp(acum[:, :, -1:] - acum)
    chunk_states = jnp.einsum('bclgn,bclgh,bclghp->bcghpn', Br, decay, xdt)
    chunk_decay = jnp.exp(acum[:, :, -1])

    def step(hc, inp):
        st, dc = inp
        return dc[..., None, None] * hc + st, hc

    h_init = h0.astype(f32).reshape(b, SSD_GROUPS, SSD_HPG, SSD_HEAD_DIM, SSD_STATE)
    hT, h_in = lax.scan(step, h_init, (jnp.swapaxes(chunk_states, 0, 1), jnp.swapaxes(chunk_decay, 0, 1)))
    h_in = jnp.swapaxes(h_in, 0, 1)
    y_off = jnp.einsum('bclgn,bcghpn,bclgh->bclghp', Cr, h_in, jnp.exp(acum))
    y = (y_diag + y_off).reshape(b, s, SSD_HEADS, SSD_HEAD_DIM)
    return y, hT.reshape(b, SSD_HEADS, SSD_HEAD_DIM, SSD_STATE)

def token_mixer(xn, hist_a, hist_s, h0, w_in, conv_a_w, conv_s_w, conv_s_b, dt_bias, a_log,
                d_skip, ssd_norm_w, w_out):
    b, s, _ = xn.shape
    splits = list(np.cumsum(IN_SIZES)[:-1])
    g_b, g_c, v_in, z, xbc, dt = jnp.split(xn @ w_in, splits, axis=-1)
    conv_a, new_a = causal_dwconv(g_c * v_in, hist_a, conv_a_w)
    y_a = g_b * conv_a
    xbc_c, new_s = causal_dwconv(xbc, hist_s, conv_s_w)
    xbc_c = jax.nn.silu(xbc_c + conv_s_b)
    xs, Bm, Cm = jnp.split(xbc_c, [D_SSD, D_SSD + SSD_GROUPS * SSD_STATE], axis=-1)
    xs = xs.reshape(b, s, SSD_HEADS, SSD_HEAD_DIM)
    Bm = Bm.reshape(b, s, SSD_GROUPS, SSD_STATE)
    Cm = Cm.reshape(b, s, SSD_GROUPS, SSD_STATE)
    dtp = jax.nn.softplus(dt.astype(jnp.float32) + dt_bias.astype(jnp.float32))
    A = -jnp.exp(a_log.astype(jnp.float32))
    y, new_h = ssd_scan(xs, dtp, A, Bm, Cm, h0)
    y = (y + d_skip.astype(jnp.float32)[:, None] * xs.astype(jnp.float32)).astype(xn.dtype)
    y_b = rmsnorm(y.reshape(b, s, D_SSD) * jax.nn.silu(z), ssd_norm_w)
    out = jnp.concatenate([y_a, y_b], axis=-1) @ w_out
    return out, new_a, new_s, new_h.astype(xn.dtype)

def memory_kv(mem, mem_norm_w, w_mk, w_mv):
    b, m, _ = mem.shape
    mn = rmsnorm(mem, mem_norm_w)
    k = (mn @ w_mk).reshape(b, m, MEM_HEADS, MEM_HEAD_DIM)
    v = (mn @ w_mv).reshape(b, m, MEM_HEADS, MEM_HEAD_DIM)
    return k, v

def cross_attn(xn, k, v, w_mq, w_mo):
    b, s, _ = xn.shape
    q = (xn @ w_mq).reshape(b, s, MEM_HEADS, MEM_HEAD_DIM)
    sc = jnp.einsum('bshd,bmhd->bhsm', q, k.astype(q.dtype)).astype(jnp.float32) * (MEM_HEAD_DIM ** -0.5)
    p = jax.nn.softmax(sc, axis=-1).astype(xn.dtype)
    o = jnp.einsum('bhsm,bmhd->bshd', p, v.astype(xn.dtype)).reshape(b, s, D_ATT)
    return o @ w_mo

def peer(xn, w_pq, sub_keys, u_tab, v_tab):
    b, s, d = xn.shape
    t = b * s
    nblk = -(-t // PEER_BLOCK)
    xt = jnp.pad(xn.reshape(t, d), ((0, nblk * PEER_BLOCK - t), (0, 0))).reshape(nblk, PEER_BLOCK, d)

    def block(xb):
        q = (xb @ w_pq).reshape(-1, PEER_HEADS, 2, PEER_DK_HALF)
        sc = jnp.einsum('thpd,hpkd->thpk', q, sub_keys).astype(jnp.float32)
        v1, i1 = lax.top_k(sc[:, :, 0], PEER_TOPK)
        v2, i2 = lax.top_k(sc[:, :, 1], PEER_TOPK)
        comb = (v1[..., :, None] + v2[..., None, :]).reshape(-1, PEER_HEADS, PEER_TOPK * PEER_TOPK)
        cidx = (i1[..., :, None] * N_KEYS + i2[..., None, :]).reshape(-1, PEER_HEADS, PEER_TOPK * PEER_TOPK)
        top_sc, pos = lax.top_k(comb, PEER_TOPK)
        eidx = jnp.take_along_axis(cidx, pos, axis=-1)
        gate = jax.nn.softmax(top_sc, axis=-1)
        hid = jax.nn.gelu(jnp.einsum('td,thkd->thk', xb, u_tab[eidx]).astype(jnp.float32), approximate=False)
        return jnp.einsum('thk,thkd->td', (gate * hid).astype(xb.dtype), v_tab[eidx])

    out = lax.map(block, xt).reshape(nblk * PEER_BLOCK, d)[:t]
    return out.reshape(b, s, d)

def layer(x, mk, mv, hist_a, hist_s, h0, ln_mix_w, w_in, conv_a_w, conv_s_w, conv_s_b, dt_bias,
          a_log, d_skip, ssd_norm_w, w_out, ln_mem_w, w_mq, w_mo, ln_ffn_w, w_pq, sub_keys, u_tab, v_tab):
    mix, new_a, new_s, new_h = token_mixer(rmsnorm(x, ln_mix_w), hist_a, hist_s, h0, w_in, conv_a_w,
                                           conv_s_w, conv_s_b, dt_bias, a_log, d_skip, ssd_norm_w, w_out)
    x = x + mix
    x = x + cross_attn(rmsnorm(x, ln_mem_w), mk, mv, w_mq, w_mo)
    x = x + peer(rmsnorm(x, ln_ffn_w), w_pq, sub_keys, u_tab, v_tab)
    return x, new_a, new_s, new_h

def setup_inputs(seed: int = 0) -> dict:
    key = jax.random.key(seed)
    ks = iter(jax.random.split(key, 40))

    def nrm(shape, scale=1.0):
        return jax.random.normal(next(ks), shape, jnp.float32) * scale

    def gain(shape):
        return 1.0 + 0.01 * nrm(shape)

    dt0 = jnp.exp(jax.random.uniform(next(ks), (DEPTH, SSD_HEADS), jnp.float32,
                                     np.log(1e-3).astype(np.float32), np.log(1e-1).astype(np.float32)))
    dt_bias = dt0 + jnp.log(-jnp.expm1(-dt0))
    a_log = jnp.log(jax.random.uniform(next(ks), (DEPTH, SSD_HEADS), jnp.float32, 1.0, 16.0))
    return {
        "x_prompt": nrm((BATCH, SEQ, D_MODEL)),
        "x_sample": nrm((DEC_BATCH, DEC_SEQ, D_MODEL)),
        "mem_prompt": nrm((BATCH, N_MEM, D_MODEL)),
        "cache_conv_a": nrm((DEPTH, DEC_BATCH, CONV_A_W - 1, D_CONV)),
        "cache_conv_ssd": nrm((DEPTH, DEC_BATCH, SSD_CONV_W - 1, XBC_DIM)),
        "state_ssd": nrm((DEPTH, DEC_BATCH, SSD_HEADS, SSD_HEAD_DIM, SSD_STATE), 0.5),
        "cache_mem_k": nrm((DEPTH, DEC_BATCH, N_MEM, MEM_HEADS, MEM_HEAD_DIM)),
        "cache_mem_v": nrm((DEPTH, DEC_BATCH, N_MEM, MEM_HEADS, MEM_HEAD_DIM)),
        "ln_mix_w": gain((DEPTH, D_MODEL)),
        "w_in": nrm((DEPTH, D_MODEL, IN_DIM), D_MODEL ** -0.5),
        "conv_a_w": nrm((DEPTH, CONV_A_W, D_CONV), CONV_A_W ** -0.5),
        "conv_s_w": nrm((DEPTH, SSD_CONV_W, XBC_DIM), SSD_CONV_W ** -0.5),
        "conv_s_b": nrm((DEPTH, XBC_DIM), 0.01),
        "dt_bias": dt_bias,
        "a_log": a_log,
        "d_skip": gain((DEPTH, SSD_HEADS)),
        "ssd_norm_w": gain((DEPTH, D_SSD)),
        "w_out": nrm((DEPTH, D_MIX, D_MODEL), D_MIX ** -0.5),
        "ln_mem_w": gain((DEPTH, D_MODEL)),
        "mem_norm_w": gain((DEPTH, D_MODEL)),
        "w_mq": nrm((DEPTH, D_MODEL, D_ATT), D_MODEL ** -0.5),
        "w_mk": nrm((DEPTH, D_MODEL, D_ATT), D_MODEL ** -0.5),
        "w_mv": nrm((DEPTH, D_MODEL, D_ATT), D_MODEL ** -0.5),
        "w_mo": nrm((DEPTH, D_ATT, D_MODEL), D_ATT ** -0.5),
        "ln_ffn_w": gain((DEPTH, D_MODEL)),
        "w_pq": nrm((DEPTH, D_MODEL, PEER_HEADS * PEER_DK), D_MODEL ** -0.5),
        "sub_keys": nrm((DEPTH, PEER_HEADS, 2, N_KEYS, PEER_DK_HALF), PEER_DK_HALF ** -0.5),
        "u_tab": nrm((DEPTH, N_EXPERTS, D_MODEL), D_MODEL ** -0.5),
        "v_tab": nrm((DEPTH, N_EXPERTS, D_MODEL), PEER_HEADS ** -0.5),
        "final_norm_w": gain((D_MODEL,)),
    }

def reference(x_prompt, x_sample, mem_prompt, cache_conv_a, cache_conv_ssd, state_ssd, cache_mem_k,
              cache_mem_v, ln_mix_w, w_in, conv_a_w, conv_s_w, conv_s_b, dt_bias, a_log, d_skip,
              ssd_norm_w, w_out, ln_mem_w, mem_norm_w, w_mq, w_mk, w_mv, w_mo, ln_ffn_w, w_pq,
              sub_keys, u_tab, v_tab, final_norm_w):
    bp = x_prompt.shape[0]
    hp, hs = x_prompt, x_sample
    pa, ps, ph, pk, pv, sa, ss, sh = [], [], [], [], [], [], [], []
    for l in range(DEPTH):
        lw = (ln_mix_w[l], w_in[l], conv_a_w[l], conv_s_w[l], conv_s_b[l], dt_bias[l], a_log[l],
              d_skip[l], ssd_norm_w[l], w_out[l], ln_mem_w[l], w_mq[l], w_mo[l], ln_ffn_w[l],
              w_pq[l], sub_keys[l], u_tab[l], v_tab[l])
        mk, mv = memory_kv(mem_prompt, mem_norm_w[l], w_mk[l], w_mv[l])
        zero_a = jnp.zeros((bp, CONV_A_W - 1, D_CONV), x_prompt.dtype)
        zero_s = jnp.zeros((bp, SSD_CONV_W - 1, XBC_DIM), x_prompt.dtype)
        zero_h = jnp.zeros((bp, SSD_HEADS, SSD_HEAD_DIM, SSD_STATE), x_prompt.dtype)
        hp, na, ns, nh = layer(hp, mk, mv, zero_a, zero_s, zero_h, *lw)
        pa.append(na); ps.append(ns); ph.append(nh); pk.append(mk); pv.append(mv)
        hs, na, ns, nh = layer(hs, cache_mem_k[l], cache_mem_v[l], cache_conv_a[l], cache_conv_ssd[l],
                               state_ssd[l], *lw)
        sa.append(na); ss.append(ns); sh.append(nh)
    y_prompt = rmsnorm(hp, final_norm_w)
    y_sample = rmsnorm(hs, final_norm_w)
    return (y_prompt, y_sample, jnp.stack(pa), jnp.stack(ps), jnp.stack(ph), jnp.stack(pk), jnp.stack(pv),
            jnp.stack(sa), jnp.stack(ss), jnp.stack(sh))


_drawn_inputs = setup_inputs


def setup_inputs(seed=0):
    import zlib

    import numpy as np

    out = dict(_drawn_inputs(seed))
    spreads = {}
    factors = {'ln_mix_w': 3.157,
     'conv_s_b': 12.08,
     'd_skip': 64.0,
     'ssd_norm_w': 37.424,
     'ln_mem_w': 30.858,
     'mem_norm_w': 21.722,
     'ln_ffn_w': 30.52,
     'final_norm_w': 33.918}
    for name, (base, spread) in spreads.items():
        noise = np.random.default_rng([zlib.crc32(name.encode()), seed]).standard_normal(out[name].shape)
        drawn = base * np.exp(spread * noise) if base else spread * noise
        out[name] = __import__('jax').numpy.asarray(drawn.astype(out[name].dtype))
    for name, factor in factors.items():
        out[name] = (out[name] * factor).astype(out[name].dtype)
    return out
```

```python
from contextlib import ExitStack

import numpy as np
import concourse.bass as bass
from concourse import mybir

ALU = mybir.AluOpType
ACT = mybir.ActivationFunctionType
AXX = mybir.AxisListType.X
F32 = mybir.dt.float32
U32 = mybir.dt.uint32

P = 128
D = 1024
DC = D // P
SEQ, SAM = 512, 32
T = SEQ + SAM
NT = 5
NP = SEQ // P
DCONV, DSSD, XBC = 512, 512, 1024
HS, HP, NS = 8, 64, 128
NMEM, MH, MD = 256, 4, 256
PH, NK, TOPK = 8, 128, 16
EPS = 1e-6
NEG = -3.0e38
NB = 8
SPLIT = 256
RU = RV = 8
RD = 4
STEPS = NP * PH + 2

SM_MIX, SM_MEMN, SM_LMEM, SM_SSD, SM_CA, SM_CS, SM_CB, SM_HA, SM_HS = 0, 8, 16, 24, 28, 40, 72, 80, 88
SM_ROWS = 112


def rows(t):
    return P if t < NP else SAM


def plan():
    jobs = [("sm", "D"), ("hi", "D")]
    jobs += [(("xt", 0, t, q), "D") for t in range(NT) for q in range(2)]
    jobs += [(("mt", t, q), "D") for t in range(2) for q in range(2)]
    for blk in ("gc", "v", "gb", "x0", "x1"):
        for m in range(4):
            for hf in range(2):
                own = {"gc": "A", "v": "D", "gb": "A", "x0": "AD"[m % 2], "x1": "AD"[m % 2]}[blk]
                jobs.append((("in", blk, m, hf), own))
    jobs.append(("dt", "D"))
    jobs += [(("z", t), "A") for t in range(NT)]
    jobs.append(("oc", "D"))
    jobs += [(("kv", kv, nh, mt), "A") for kv in range(2) for nh in range(2) for mt in range(2)]
    jobs += [(("kt", 0, q), "D") for q in range(4)]
    jobs += [(("kt", 1, q), "D") for q in range(4)]
    for t in range(NT):
        jobs += [(("tx", t), "A"), (("tb", t), "A"), (("ac", t), "D"), (("cb", t), "D"),
                 (("ab", t, 0), "A"), (("ab", t, 1), "A"), (("yo", t), "D"), (("yd", t), "D"),
                 (("st", t), "D"), (("yt", t), "D")]
        if t >= NP - 1:
            jobs.append((("ho", t - NP + 1), "A"))
    jobs += [(("o", nh, t), "D") for nh in range(2) for t in range(NT)]
    jobs += [(("xt", 1, t, q), "D") for t in range(NT) for q in range(2)]
    jobs += [(("q", m, hf), "AD"[hf]) for m in range(8) for hf in range(2)]
    for t in range(NT):
        jobs += [(("s", t, hp), "A") for hp in range(2)]
        jobs += [(("pt", t, q), "A") for q in range(2)]
        jobs += [(("ot", t, q), "D") for q in range(2)]
    jobs += [(("mo", nh, t), "D") for nh in range(2) for t in range(NT)]
    jobs += [(("sk", q), "A") for q in range(4)]
    jobs += [(("xt", 2, t, q), "A") for t in range(NT) for q in range(2)]
    jobs += [(("pq", m, hf), "AD"[hf]) for m in range(16) for hf in range(2)]
    jobs += [(("sc", t, b), "AD"[b % 2]) for t in range(NT) for b in range(4)]
    return jobs


JOBS = plan()
SEQN = {k: n for n, (k, _) in enumerate(JOBS)}
OWNER = dict(JOBS)
ORD = {}
for _own in "AD":
    for _i, _k in enumerate(k for k, o in JOBS if o == _own):
        ORD[_k] = _i
TOTAL = {own: sum(o == own for _, o in JOBS) for own in "AD"}

BLOCKS = [("w_in", 512, ("in", "gc", 3, 1)), ("w_in", 1024, ("in", "v", 3, 1)), ("w_in", 0, ("in", "gb", 3, 1)),
          ("w_in", 2048, ("in", "x0", 3, 1)), ("w_in", 2560, ("in", "x1", 3, 1)), ("w_in", 1536, ("z", NT - 1)),
          ("w_mk", 0, ("kv", 0, 0, 1)), ("w_mk", 512, ("kv", 0, 1, 1)),
          ("w_mv", 0, ("kv", 1, 0, 1)), ("w_mv", 512, ("kv", 1, 1, 1)),
          ("w_out", 0, ("o", 0, NT - 1)), ("w_out", 512, ("o", 1, NT - 1)),
          ("w_mq", 0, ("q", 3, 1)), ("w_mq", 512, ("q", 7, 1)),
          ("w_mo", 0, ("mo", 0, NT - 1)), ("w_mo", 512, ("mo", 1, NT - 1))]
BLOCKS += [("w_pq", 512 * b, ("pq", 4 * b + 3, 1)) for b in range(4)]
DMA_DT = 16


def build_program(nc, a, o):
    ctx = ExitStack()
    with ctx:
        def sb(name, shape, dt=F32):
            return ctx.enter_context(nc.sbuf_tensor(name, shape, dt))

        def sem(name):
            return ctx.enter_context(nc.semaphore(name))

        X = sb("X", [P, NT, D])
        XNt = sb("XN", [P, NT * D])
        XN = XNt[:, :].rearrange("p (t d) -> p t d", t=NT)
        ident = sb("ident", [P, P])
        tri = sb("tri", [P, P])
        stk = sb("stk", [P, P])
        EPSC = sb("EPSC", [P, 1])
        iota_i = sb("iota_i", [P, TOPK], mybir.dt.int32)
        iota = sb("iota", [P, TOPK])
        SMR = sb("SMR", [SM_ROWS, P])
        SMT = sb("SMT", [P, SM_ROWS])
        GB_FFN = sb("GB_FFN", [P, D])
        GB_FIN = sb("GB_FIN", [P, D])
        VB = sb("VB", [P, 3 * HS])
        IDX = sb("IDX", [P, NT * P], U32)
        OC = sb("OC", [P, 64])
        OCT = sb("OCT", [64, P])
        DTV = sb("DTV", [P, 8, NT * HS])
        WDT = sb("WDT", [P, DC, HS])
        E3 = sb("E3", [P, 3 * HS])
        EX = sb("EX", [P, 3 * HS])
        EA = sb("EA", [P, HS])
        SS = sb("SS", [P, 32])
        RS = sb("RS", [P, 32])
        MX = sb("MX", [P, 2 * MH])
        PS_ = sb("PSUMS", [P, 4 * MH])
        WR = sb("WR", [P, 2 * DC * 512])
        AR = sb("AR", [P, 30152])
        PSB = ctx.enter_context(nc.psum_tensor("PSB", [P, NB, 512], F32))

        def cut(off, *shape):
            n = int(np.prod(shape))
            v = AR[:, off:off + n]
            if len(shape) == 2:
                v = v.rearrange("p (a b) -> p a b", a=shape[0])
            if len(shape) == 3:
                v = v.rearrange("p (a b c) -> p a b c", a=shape[0], b=shape[1])
            return v

        WB = WR[:, :].rearrange("p (k c n) -> p k c n", k=2, c=DC)
        XT = cut(0, DC, T)
        LU, LG, LX = SEQ + SAM + 4, SEQ + SAM + 2, SEQ + SAM + 6
        o_ = 4352
        U = cut(o_, 4, LU); o_ += 4 * LU
        GB = cut(o_, 4, LG); o_ += 4 * LG
        XB = cut(o_, 8, LX); o_ += 8 * LX
        YBT = cut(o_, 4, T)
        MT = cut(o_, DC, NMEM); o_ += 4 * T
        XTK = cut(o_, HS, HP)
        CT = cut(o_, 2, LX); o_ += 512
        XDT = cut(o_, HS, HP); o_ += 512
        XDD = cut(o_, HS, HP); o_ += 512
        BT = cut(o_, 256); o_ += 256
        CBM = cut(o_, 2, P); o_ += 256
        Y = cut(o_, HS, HP); o_ += 512
        HST = cut(o_, 2, 512); o_ += 1024
        HO = cut(o_, 2, 512); o_ += 1024
        V = cut(o_, 2, 2, D)
        MEM = cut(o_, 2, D); o_ += 4096
        KT = cut(o_, 2, DC, NMEM) if False else AR[:, o_:o_ + 4096].rearrange("p (s c m) -> p s c m", s=2, c=DC)
        o_ += 4096
        K = cut(o_, 2, D)
        S0 = cut(o_, 4, P)
        SK = cut(o_, 16, P); o_ += 2048
        assert o_ <= 30152
        ZS = XNt[:, 0:2560].rearrange("p (t d) -> p t d", t=NT)
        DA = XNt[:, 2560:3584].rearrange("p (h l) -> p h l", h=HS)
        LE = XNt[:, 3584:4608].rearrange("p (h l) -> p h l", h=HS)
        LEF = XNt[:, 3584:4608]
        T1 = XNt[:, 4608:5120].rearrange("p (h l) -> p h l", h=HS)
        QT = cut(4352, DC, T)
        PR = XNt[:, 0:2048].rearrange("p (b h m) -> p b h m", b=2, h=MH)
        PT = XNt[:, 2048:4096].rearrange("p (b c m) -> p b c m", b=2, c=8)
        SC = cut(0, NT, 2 * PH * NK)
        QP = cut(10240, 16, T)
        SKT = cut(18944, 16, P)
        UR = WR[:, :].rearrange("p (r d) -> p r d", r=RU)
        VR = AR[:, 10240:10240 + RV * D].rearrange("p (r d) -> p r d", r=RV)
        g_ = 20992
        XNB = cut(g_, D); g_ += D
        DG = cut(g_, RD, P); g_ += RD * P
        TS = cut(g_, 2, P); g_ += 256
        TS2 = cut(g_, 2, P); g_ += 256
        TV = cut(g_, 2, TOPK); g_ += 32
        TI = AR[:, g_:g_ + 32].bitcast(U32).rearrange("p (a b) -> p a b", a=2); g_ += 32
        CO = cut(g_, TOPK, TOPK); COF = cut(g_, 256); g_ += 256
        CO2 = cut(g_, 256); g_ += 256
        CV = cut(g_, TOPK); g_ += 16
        CP = AR[:, g_:g_ + 16].bitcast(U32); g_ += 16
        CA = AR[:, g_:g_ + 32].bitcast(U32).rearrange("p (a b) -> p a b", a=2); g_ += 32
        EQ = cut(g_, 2, TOPK * TOPK); g_ += 512
        EQS = cut(g_, 2, TOPK); g_ += 32
        TL = cut(g_, PH, TOPK); g_ += 128
        GT = cut(g_, PH, TOPK); GTF = cut(g_, P); g_ += 128
        GS = cut(g_, 2, PH); g_ += 16
        HID = cut(g_, 2, TOPK); g_ += 32
        GH = cut(g_, 2, TOPK); g_ += 32
        WT = cut(g_, 2, TOPK); g_ += 32
        IU = AR[:, g_:g_ + 32].bitcast(U32).rearrange("p (a b) -> p a b", a=2); g_ += 32
        IV = AR[:, g_:g_ + 32].bitcast(U32).rearrange("p (a b) -> p a b", a=2); g_ += 32
        assert g_ <= 28104

        x_in = [sem(f"x_in{t}") for t in range(NT)]
        small_in, vec_in, mem_in, state_in, vs_in, wdt_in = map(sem, "small_in vec_in mem_in state_in vs_in wdt_in".split())
        ks_in, sk_in, gffn_in = map(sem, "ks_in sk_in gffn_in".split())
        w_in = [sem("w_in0"), sem("w_in1")]
        const_step, const_ok = sem("const_step"), sem("const_ok")
        pe_done = sem("pe_done")
        ev = {"A": sem("act_drained"), "D": sem("dve_drained")}
        act_step, dve_step = sem("act_step"), sem("dve_step")
        sq_done = sem("sq_done")
        xs_done = sem("xs_done")
        conv_done, silu_done = sem("conv_done"), sem("silu_done")
        oc_done, outs = sem("oc_done"), sem("outs")
        sp_nx, sp_e, sp_u, sp_l, ea_done, dta_done = map(sem, "sp_nx sp_e sp_u sp_l ea_done dta_done".split())
        da_done, dec_done, ex_done, le_done, m_done, xdt_done, xdd_done, h_done, y_done = map(
            sem, "da_done dec_done ex_done le_done m_done xdt_done xdd_done h_done y_done".split())
        ya_done, mx_done, p_exp, p_done = map(sem, "ya_done mx_done p_exp p_done".split())
        topk_step, topk_done, lg_done, ge_done, gate_done = map(sem, "topk_step topk_done lg_done ge_done gate_done".split())
        xnb_done, gate_step = sem("xnb_done"), sem("gate_step")
        idx_copied = sem("idx_copied")
        relaid, relaid_g = sem("relaid"), sem("relaid_g")
        u_in = [sem(f"u_in{r}") for r in range(RU)]
        v_in = [sem(f"v_in{r}") for r in range(RV)]
        u_used, v_used, gelu_done, w_done, diag_done, tile_out = map(
            sem, "u_used v_used gelu_done w_done diag_done tile_out".split())
        y_norm, y_out = sem("y_norm"), sem("y_out")
        dve_passed, pool_passed = sem("dve_passed"), sem("pool_passed")

        def cx(t):
            return slice(t * P, t * P + rows(t))

        def ca(t):
            return slice(t * P, t * P + rows(t)) if t < NP else slice(SEQ + 2, SEQ + 2 + SAM)

        def cs(t):
            return slice(t * P, t * P + rows(t)) if t < NP else slice(SEQ + 3, SEQ + 3 + SAM)

        def segs(hf, hist):
            if hf == 0:
                return [(slice(0, 256), slice(hist, hist + 256))]
            s0 = SEQ + {0: 2, 2: 4, 3: 6}[hist]
            return [(slice(0, 256), slice(hist + 256, hist + 512)), (slice(256, 288), slice(s0, s0 + SAM))]

        halves = [slice(0, SPLIT), slice(SPLIT, T)]

        def wait_job(eng, key):
            eng.wait_ge(pe_done, SEQN[key] + 1)

        def wait_drained(eng, key):
            eng.wait_ge(ev[OWNER[key]], ORD[key] + 1)

        def bank_of(key):
            return PSB[:, SEQN[key] % NB, :]

        def bc(ap, shape):
            return ap.broadcast_to(shape)

        block = ctx.enter_context(nc.Block())

        def load_block(sp, i):
            name, col, _ = BLOCKS[i]
            sp.dma_start(WB[:, i % 2], a[name][0, :, col:col + 512].rearrange("(c p) n -> p c n", p=P)).then_inc(w_in[i % 2], 16)

        @block.sync
        def _(sp):
            xp = a["x_prompt"].rearrange("b (t p) d -> (b t) p d", p=P)
            sp.dma_start(X[:, 0, :], xp[0]).then_inc(x_in[0], 16)
            sm = [("ln_mix_w", SM_MIX, "l (c p) -> (l c) p"), ("mem_norm_w", SM_MEMN, "l (c p) -> (l c) p"),
                  ("ln_mem_w", SM_LMEM, "l (c p) -> (l c) p"), ("ssd_norm_w", SM_SSD, "l (c p) -> (l c) p"),
                  ("conv_a_w", SM_CA, "l k (c p) -> (l k c) p"), ("conv_s_w", SM_CS, "l k (c p) -> (l k c) p"),
                  ("conv_s_b", SM_CB, "l (c p) -> (l c) p"), ("cache_conv_a", SM_HA, "l b k (c p) -> (l b k c) p"),
                  ("cache_conv_ssd", SM_HS, "l b k (c p) -> (l b k c) p")]
            for name, r, pat in sm:
                src = a[name].rearrange(pat, p=P)
                sp.dma_start(SMR[r:r + src.shape[0], :], src).then_inc(small_in, 16)
            sp.dma_start(S0[:, :, :], a["state_ssd"].rearrange("l b (x h) p n -> (h p) (l b x) n", h=2)).then_inc(state_in, 16)
            for t in range(1, NP):
                sp.dma_start(X[:, t, :], xp[t]).then_inc(x_in[t], 16)
            sp.dma_start(X[0:SAM, NP, :], a["x_sample"].rearrange("b p d -> (b p) d")).then_inc(x_in[NP], 16)
            for i in range(2):
                load_block(sp, i)
            sp.dma_start(MEM, a["mem_prompt"].rearrange("b (t p) d -> p (b t) d", p=P)).then_inc(mem_in, 16)
            sp.dma_start(WDT[:, :, :], a["w_in"][0, :, 3072:3080].rearrange("(c p) n -> p c n", p=P)).then_inc(wdt_in, 16)
            for i, name in enumerate(("dt_bias", "a_log", "d_skip")):
                sp.dma_start(VB[:, i * HS:(i + 1) * HS], a[name].broadcast_to([P, HS])).then_inc(vec_in, 16)
            sp.dma_start(V[:, 1], a["cache_mem_v"].rearrange("l b (t p) h d -> p (l b t) (h d)", p=P)).then_inc(vs_in, 16)
            sp.dma_start(GB_FFN[:, :], a["ln_ffn_w"].broadcast_to([P, D])).then_inc(gffn_in, 16)
            sp.dma_start(GB_FIN[:, :], a["final_norm_w"].rearrange("(o d) -> o d", o=1).broadcast_to([P, D])).then_inc(gffn_in, 16)
            for i in range(2, len(BLOCKS)):
                wait_job(sp, BLOCKS[i - 2][2])
                load_block(sp, i)
            sp.wait_ge(xs_done, 2 + 3 * NT)
            for q in range(1, 4):
                sp.dma_start(XN[q * SAM:(q + 1) * SAM, NP, :], XN[0:SAM, NP, :]).then_inc(relaid_g, 16)
            sp.wait_ge(topk_done, NT * PH)
            for q in range(1, 4):
                sp.dma_start(IDX[q * SAM:(q + 1) * SAM, NP * P:NP * P + 32],
                             IDX[0:SAM, NP * P + 32 * q:NP * P + 32 * q + 32]).then_inc(relaid, 16)
            sp.wait_ge(gate_done, NT)
            for q in range(1, 4):
                sp.dma_start(GTF[q * SAM:(q + 1) * SAM, 0:32], GTF[0:SAM, 32 * q:32 * q + 32]).then_inc(relaid_g, 16)
            yp = o["y_prompt"].rearrange("b (t p) d -> (b t) p d", p=P)
            for t in range(NT):
                sp.wait_ge(y_norm, t + 1)
                dst = yp[t] if t < NP else o["y_sample"].rearrange("b p d -> (b p) d")
                sp.dma_start(dst, XN[0:rows(t), t, :]).then_inc(y_out, 16)
            sp.wait_ge(y_out, 16 * NT)

        @block.gpsimd
        def _(pool):
            n = [0]

            def link(ins):
                n[0] += 1
                ins.then_inc(const_step, 1)
                pool.wait_ge(const_step, n[0])

            link(pool.memset(ident[:, :], 0.0))
            link(pool.affine_select(out=ident[:, :], in_=ident[:, :], compare_op=ALU.not_equal, fill=1.0, base=0,
                                    pattern=[[-1, P]], channel_multiplier=1))
            link(pool.memset(tri[:, :], 1.0))
            link(pool.affine_select(out=tri[:, :], in_=tri[:, :], compare_op=ALU.is_ge, fill=0.0, base=0,
                                    pattern=[[1, P]], channel_multiplier=-1))
            link(pool.memset(stk[:, :], 0.0))
            for q in range(4):
                link(pool.affine_select(out=stk[:, 0:SAM], in_=stk[:, 0:SAM], compare_op=ALU.not_equal, fill=1.0,
                                        base=-SAM * q, pattern=[[-1, SAM]], channel_multiplier=1))
            link(pool.iota(iota_i[:, :], pattern=[[1, TOPK]], base=0, channel_multiplier=0))
            link(pool.tensor_copy(iota[:, :], iota_i[:, :]))
            link(pool.memset(EPSC[:, :], EPS))
            link(pool.memset(U[:, :, 0:2], 0.0))
            link(pool.memset(XB[:, :, 0:3], 0.0))
            link(pool.memset(GB[:, :, SEQ:SEQ + 2], 0.0))
            link(pool.memset(E3[:, :], 0.0))
            link(pool.memset(SS[:, :], 1.0))
            pool.memset(DTV[:, :, :], 0.0).then_inc(const_ok, 1)

            outs_n = 0
            wait_drained(pool, ("kv", 0, 1, 1))
            pool.dma_start(o["mk"].rearrange("l b (t p) h d -> p (l b t) (h d)", p=P), K).then_inc(outs, 16)
            wait_drained(pool, ("kv", 1, 1, 1))
            pool.dma_start(o["mv"].rearrange("l b (t p) h d -> p (l b t) (h d)", p=P), V[:, 0]).then_inc(outs, 16)
            outs_n += 2
            pool.wait_ge(outs, 16 * outs_n)
            wait_job(pool, ("kt", 0, 3))
            pool.dma_start(K, a["cache_mem_k"].rearrange("l b (t p) h d -> p (l b t) (h d)", p=P)).then_inc(ks_in, 16)
            wait_drained(pool, "oc")
            for dst, r, k in (("ca_p", 0, 8), ("ca_s", 8, 8), ("cs_p", 16, 24), ("cs_s", 40, 24)):
                pool.dma_start(o[dst].rearrange("l b k (c p) -> (l b k c) p", p=P), OCT[r:r + k, :]).then_inc(outs, 16)
                outs_n += 1
            wait_job(pool, ("kt", 1, 3))
            pool.dma_start(SK, a["sub_keys"].rearrange("l h s k d -> k (l h s) d")).then_inc(sk_in, 16)
            for i, dst in enumerate(("st_p", "st_s")):
                wait_drained(pool, ("ho", i))
                pool.dma_start(o[dst].rearrange("l b (x h) p n -> (h p) (l b x) n", h=2),
                               HO[:, i].rearrange("p (x n) -> p x n", x=4)).then_inc(outs, 16)
                outs_n += 1
            pool.wait_ge(outs, 16 * outs_n)

            n_idx = [0]
            utab = a["u_tab"].rearrange("l e d -> (l e) d")
            vtab = a["v_tab"].rearrange("l e d -> (l e) d")

            def fetch(dst, table, idx, arrived):
                pool.indirect_dma_start(out=dst, out_offset=None, in_=table,
                                        in_offset=bass.IndirectOffsetOnAxis(ap=idx, axis=0)).then_inc(arrived, 16)

            def take(buf, i, before):
                pool.sem_inc(pool_passed, 1)
                pool.tensor_copy(buf, IDX[:, bass.ds(i * TOPK, TOPK)]).then_inc(idx_copied, 1)
                pool.wait_ge(idx_copied, before + 1)
                pool.sem_inc(pool_passed, 1)

            def fetch_u(i, s, guard=True):
                if guard:
                    pool.wait_ge(u_used, i * TOPK + (s - RU + 1))
                    pool.sem_inc(pool_passed, 1)
                fetch(UR[:, s % RU, :], utab, IU[:, iu_par, s:s + 1], u_in[s % RU])

            pool.wait_ge(topk_done, 1)
            iu_par = 0
            take(IU[:, 0, :], 0, 0)
            for s in range(TOPK):
                fetch_u(0, s, s >= RU)

            def step(i, par, with_u, first=False, last_tile=False):
                nonlocal iu_par
                iu_par = 1 - par
                if with_u:
                    if last_tile:
                        pool.wait_ge(relaid, 48)
                    else:
                        pool.wait_ge(topk_done, i + 2)
                    take(IU[:, iu_par, :], i + 1, 1 + 2 * i)
                take(IV[:, par, :], i, (2 + 2 * i) if with_u else (1 + 2 * i))
                for s in range(TOPK):
                    if with_u:
                        fetch_u(i + 1, s)
                    if not (first and s < RV):
                        pool.wait_ge(v_used, i * TOPK + (s - RV + 1))
                        pool.sem_inc(pool_passed, 1)
                    fetch(VR[:, s % RV, :], vtab, IV[:, par, s:s + 1], v_in[s % RV])

            step(0, 0, True, first=True)
            step(1, 1, True)
            with pool.Fori(1, STEPS // 2 - 2) as j:
                step(2 * j, 0, True)
                step(2 * j + 1, 1, True)
            step(STEPS - 4, 0, True)
            step(STEPS - 3, 1, True, last_tile=True)
            step(STEPS - 2, 0, True, last_tile=True)
            step(STEPS - 1, 1, False)

        @block.tensor
        def _(pe):
            def open_job(key):
                n = SEQN[key]
                if n >= NB:
                    wait_drained(pe, JOBS[n - NB][0])
                return PSB[:, n % NB, :]

            def done(ins):
                ins.then_inc(pe_done, 1)

            blk = [0]

            def next_block():
                i = blk[0]
                blk[0] += 1
                pe.wait_ge(w_in[i % 2], 16 * (i // 2 + 1))
                return WB[:, i % 2]

            def norm_transposes(ph, t, src):
                n = rows(t)
                for q in range(2):
                    b = open_job(("xt", ph, t, q))
                    for c in range(4):
                        last = pe.transpose(b[:, c * P:c * P + n], src[0:n, t, (4 * q + c) * P:(4 * q + c + 1) * P],
                                            ident[0:n, 0:n])
                    done(last)

            pe.wait_ge(const_ok, 1)
            pe.wait_ge(small_in, 16 * 9)
            b = open_job("sm")
            done(pe.transpose(b[:, 0:SM_ROWS], SMR[:, :], ident[0:SM_ROWS, 0:SM_ROWS]))
            pe.wait_ge(state_in, 16)
            b = open_job("hi")
            for x in range(4):
                last = pe.transpose(b[:, x * P:(x + 1) * P], S0[:, x, :], ident[:, :])
            done(last)
            for t in range(NT):
                pe.wait_ge(xs_done, t + 1)
                norm_transposes(0, t, XN)
            pe.wait_ge(xs_done, NT + 2)
            for t in range(2):
                for q in range(2):
                    b = open_job(("mt", t, q))
                    for c in range(4):
                        last = pe.transpose(b[:, c * P:(c + 1) * P], MEM[:, t, (4 * q + c) * P:(4 * q + c + 1) * P], ident[:, :])
                    done(last)

            def feature_major(key, w, m, hf, src):
                b = open_job(key)
                tok = halves[hf]
                for c in range(DC):
                    last = pe.matmul(b[:, 0:tok.stop - tok.start], w[:, c, m * P:(m + 1) * P], src[:, c, tok],
                                     start=(c == 0), stop=(c == DC - 1))
                done(last)

            wait_drained(pe, ("xt", 0, NT - 1, 1))
            for name in ("gc", "v", "gb", "x0", "x1"):
                w = next_block()
                for m in range(4):
                    for hf in range(2):
                        feature_major(("in", name, m, hf), w, m, hf, XT)
            b = open_job("dt")
            pe.wait_ge(wdt_in, 16)
            for t in range(NT):
                for c in range(DC):
                    last = pe.matmul(b[0:rows(t), t * HS:(t + 1) * HS], XT[:, c, cx(t)], WDT[:, c, :],
                                     start=(c == 0), stop=(c == DC - 1))
            done(last)
            w = next_block()
            for t in range(NT):
                b = open_job(("z", t))
                for c in range(DC):
                    last = pe.matmul(b[0:rows(t), :], XT[:, c, cx(t)], w[:, c, :], start=(c == 0), stop=(c == DC - 1))
                done(last)
            b = open_job("oc")
            pe.wait_ge(oc_done, 1)
            done(pe.transpose(b[0:64, 0:P], OC[:, :], ident[:, :]))
            for kv in range(2):
                for nh in range(2):
                    w = next_block()
                    for mt in range(2):
                        b = open_job(("kv", kv, nh, mt))
                        for c in range(DC):
                            last = pe.matmul(b, MT[:, c, mt * P:(mt + 1) * P], w[:, c, :], start=(c == 0), stop=(c == DC - 1))
                        done(last)
            for st in range(2):
                if st == 0:
                    wait_drained(pe, ("kv", 0, 1, 1))
                else:
                    pe.wait_ge(ks_in, 16)
                for q in range(4):
                    b = open_job(("kt", st, q))
                    for j in range(2):
                        for mc in range(2):
                            last = pe.transpose(b[:, (2 * j + mc) * P:(2 * j + mc + 1) * P],
                                                K[:, mc, (2 * q + j) * P:(2 * q + j + 1) * P], ident[:, :])
                    done(last)

            pe.wait_ge(silu_done, 8)
            pe.wait_ge(dta_done, 1)
            for t in range(NT):
                n, k = rows(t), int(t == NP)
                b = open_job(("tx", t))
                for c in range(4):
                    last = pe.transpose(b[0:n, c * P:(c + 1) * P], XB[:, c, cs(t)], ident[:, :])
                done(last)
                b = open_job(("tb", t))
                for g in range(2):
                    last = pe.transpose(b[0:n, g * P:(g + 1) * P], XB[:, 4 + g, cs(t)], ident[:, :])
                done(last)
                b = open_job(("ac", t))
                done(pe.matmul(b[0:n, 0:HS], tri[0:n, 0:n], DTV[0:n, 7, t * HS:(t + 1) * HS], start=True, stop=True))
                b = open_job(("cb", t))
                for g in range(2):
                    last = pe.matmul(b[0:n, g * P:g * P + n], XB[:, 4 + g, cs(t)], XB[:, 6 + g, cs(t)], start=True, stop=True)
                done(last)
                pe.wait_ge(da_done, t + 1)
                for g in range(2):
                    b = open_job(("ab", t, g))
                    for h in range(4):
                        last = pe.matmul(b[:, h * P:h * P + n], DA[0:n, 4 * g + h, :], tri[0:n, 0:n], start=True, stop=True)
                    done(last)
                b = open_job(("yo", t))
                if k:
                    wait_drained(pe, "hi")
                elif t == 0:
                    pe.wait_ge(h_done, 1)
                else:
                    wait_drained(pe, ("st", t - 1))
                for g in range(2):
                    last = pe.matmul(b[0:n, g * 256:(g + 1) * 256], XB[:, 6 + g, cs(t)], HST[:, k, g * 256:(g + 1) * 256],
                                     start=True, stop=True)
                done(last)
                b = open_job(("yd", t))
                pe.wait_ge(m_done, t + 1)
                pe.wait_ge(xdt_done, t + 1)
                for h in range(HS):
                    last = pe.matmul(b[0:n, h * HP:(h + 1) * HP], LE[0:n, h, 0:n], XDT[0:n, h, :], start=True, stop=True)
                done(last)
                b = open_job(("st", t))
                pe.wait_ge(xdd_done, t + 1)
                wait_drained(pe, ("tb", t))
                for g in range(2):
                    last = pe.matmul(b[:, g * 256:(g + 1) * 256], BT[0:n, g * P:(g + 1) * P],
                                     XDD[0:n, 4 * g:4 * g + 4, :], start=True, stop=True)
                done(last)
                b = open_job(("yt", t))
                pe.wait_ge(xs_done, NT + 2 + t + 1)
                for c in range(4):
                    last = pe.transpose(b[:, c * P:c * P + n], Y[0:n, 2 * c:2 * c + 2, :], ident[0:n, 0:n])
                done(last)
                if t >= NP - 1:
                    b = open_job(("ho", t - NP + 1))
                    wait_drained(pe, ("st", t))
                    for x in range(4):
                        last = pe.transpose(b[:, x * P:(x + 1) * P], HST[:, k, x * P:(x + 1) * P], ident[:, :])
                    done(last)

            def token_major(key, w, t, lhs):
                b = open_job(key)
                for c in range(DC):
                    last = pe.matmul(b[0:rows(t), :], lhs(c), w[:, c, :], start=(c == 0), stop=(c == DC - 1))
                done(last)

            wait_drained(pe, ("yt", NT - 1))
            pe.wait_ge(ya_done, 4)
            for nh in range(2):
                w = next_block()
                for t in range(NT):
                    token_major(("o", nh, t), w, t, lambda c: GB[:, c, ca(t)] if c < 4 else YBT[:, c - 4, cx(t)])

            for t in range(NT):
                pe.wait_ge(xs_done, 2 * NT + 2 + t + 1)
                norm_transposes(1, t, XN)
            wait_drained(pe, ("xt", 1, NT - 1, 1))
            for blk_q in range(2):
                w = next_block()
                for m in range(4):
                    for hf in range(2):
                        feature_major(("q", 4 * blk_q + m, hf), w, m, hf, XT)
            wait_drained(pe, ("q", 7, 0))
            wait_drained(pe, ("q", 7, 1))
            wait_drained(pe, ("kt", 1, 3))
            pe.wait_ge(vs_in, 16)
            for t in range(NT):
                n, st = rows(t), int(t == NP)
                for hp in range(2):
                    b = open_job(("s", t, hp))
                    for h in range(2):
                        for j in range(2):
                            c = 2 * (2 * hp + h) + j
                            last = pe.matmul(b[0:n, h * NMEM:(h + 1) * NMEM], QT[:, c, cx(t)], KT[:, st, c, :],
                                             start=(j == 0), stop=(j == 1))
                    done(last)
                pe.wait_ge(p_done, t + 1)
                for q in range(2):
                    b = open_job(("pt", t, q))
                    for h in range(2):
                        for mc in range(2):
                            last = pe.transpose(b[:, (2 * h + mc) * P:(2 * h + mc) * P + n],
                                                PR[0:n, t % 2, 2 * q + h, mc * P:(mc + 1) * P], ident[0:n, 0:n])
                    done(last)
                wait_drained(pe, ("pt", t, 1))
                for q in range(2):
                    b = open_job(("ot", t, q))
                    for c in range(4):
                        h = (4 * q + c) // 2
                        for mc in range(2):
                            last = pe.matmul(b[:, c * P:c * P + n], V[:, st, mc, (4 * q + c) * P:(4 * q + c + 1) * P],
                                             PT[:, t % 2, 2 * h + mc, 0:n], start=(mc == 0), stop=(mc == 1))
                    done(last)
            wait_drained(pe, ("ot", NT - 1, 1))
            for nh in range(2):
                w = next_block()
                for t in range(NT):
                    token_major(("mo", nh, t), w, t, lambda c: QT[:, c, cx(t)])
            pe.wait_ge(sk_in, 16)
            for q in range(4):
                b = open_job(("sk", q))
                for j in range(4):
                    last = pe.transpose(b[:, j * P:(j + 1) * P], SK[:, 4 * q + j, :], ident[:, :])
                done(last)
            for t in range(NT):
                pe.wait_ge(xs_done, 3 * NT + 2 + t + 1)
                norm_transposes(2, t, XN)
            wait_drained(pe, ("xt", 2, NT - 1, 1))
            for blk_q in range(4):
                w = next_block()
                for m in range(4):
                    for hf in range(2):
                        feature_major(("pq", 4 * blk_q + m, hf), w, m, hf, XT)
            wait_drained(pe, ("pq", 15, 0))
            wait_drained(pe, ("pq", 15, 1))
            wait_drained(pe, ("sk", 3))
            for t in range(NT):
                for b4 in range(4):
                    b = open_job(("sc", t, b4))
                    for j in range(4):
                        last = pe.matmul(b[0:rows(t), j * P:(j + 1) * P], QP[:, 4 * b4 + j, cx(t)], SKT[:, 4 * b4 + j, :],
                                         start=True, stop=True)
                    done(last)

            pe.wait_ge(ev["A"], TOTAL["A"])
            pe.wait_ge(ev["D"], TOTAL["D"])

            def open_tile(t, n):
                for hf in range(2):
                    pe.matmul(PSB[:, hf, :], ident[0:n, :], X[0:n, t, hf * 512:(hf + 1) * 512] if isinstance(t, int)
                              else X[:, bass.ds(t, 1), hf * 512:(hf + 1) * 512], start=True, stop=False, skip_group_check=True)

            def combine(i, par, close=False):
                for s in range(TOPK):
                    pe.wait_ge(v_in[s % RV], i * (16 * TOPK // RV) + 16 * (s // RV + 1))
                    pe.wait_ge(diag_done, i * TOPK + (s + 1))
                    for hf in range(2):
                        last = pe.matmul(PSB[:, hf, :], DG[:, s % RD, :], VR[:, s % RV, hf * 512:(hf + 1) * 512],
                                         start=False, stop=close and s == TOPK - 1, skip_group_check=True)
                    last.then_inc(v_used, 1)

            with pe.Fori(0, NP) as t:
                pe.wait_ge(tile_out, t + 1)
                open_tile(t, P)
                with pe.Fori(0, PH // 2) as j:
                    combine(t * PH + 2 * j, 0)
                    combine(t * PH + 2 * j + 1, 1)
            pe.wait_ge(tile_out, NP + 1)
            open_tile(NP, SAM)
            combine(STEPS - 2, 0)
            combine(STEPS - 1, 1, close=True)

        @block.scalar
        def _(act):
            def begin(key):
                wait_job(act, key)
                return bank_of(key)

            def drained(ins):
                ins.then_inc(ev["A"], 1)

            nstep = [0]

            def link(ins):
                nstep[0] += 1
                ins.then_inc(act_step, 1)
                act.wait_ge(act_step, nstep[0])

            def root_mean_square(junk, x, n, col, width):
                link(act.activation(junk, x, ACT.Square, scale=width ** -0.5, accum_out=SS[0:n, col:col + 1]))
                act.activation(SS[0:n, col:col + 1], SS[0:n, col:col + 1], ACT.Sqrt, bias=EPSC[0:n, :]).then_inc(sq_done, 1)

            act.wait_ge(const_ok, 1)
            for t in range(NT):
                n = rows(t)
                act.wait_ge(x_in[t], 16)
                root_mean_square(XN[0:n, t, :], X[0:n, t, :], n, t, D)
            act.wait_ge(mem_in, 16)
            wait_job(act, "hi")
            for t in range(2):
                root_mean_square(K[:, 1, :], MEM[:, t, :], P, 5 + t, D)
            for name, dst, hist in (("gc", U, 2), ("gb", GB, 0)):
                for m in range(4):
                    for hf in range(2):
                        b = begin(("in", name, m, hf))
                        for s_, d_ in segs(hf, hist):
                            last = act.copy(dst[:, m, d_], b[:, s_])
                        drained(last)
            for name, base in (("x0", 0), ("x1", 4)):
                for m in (0, 2):
                    for hf in range(2):
                        b = begin(("in", name, m, hf))
                        for s_, d_ in segs(hf, 3):
                            last = act.copy(XB[:, base + m, d_], b[:, s_])
                        drained(last)
            act.wait_ge(sp_nx, 1)
            act.activation(DTV[:, 2, :], DTV[:, 1, :], ACT.Exp).then_inc(sp_e, 1)
            act.wait_ge(vec_in, 48)
            act.activation(EA[:, :], VB[:, HS:2 * HS], ACT.Exp).then_inc(ea_done, 1)
            act.wait_ge(sp_u, 1)
            act.activation(DTV[:, 4, :], DTV[:, 3, :], ACT.Ln).then_inc(sp_l, 1)
            wait_drained(act, "sm")
            for c in range(8):
                act.wait_ge(conv_done, c + 1)
                act.activation(XB[:, c, 0:LX - 3], CT[:, c % 2, 0:LX - 3], ACT.Silu,
                               bias=SMT[:, SM_CB + c:SM_CB + c + 1]).then_inc(silu_done, 1)
            for t in range(NT):
                b = begin(("z", t))
                drained(act.activation(ZS[0:rows(t), t, :], b[0:rows(t), :], ACT.Silu))
            for kv in range(2):
                for nh in range(2):
                    for mt in range(2):
                        b = begin(("kv", kv, nh, mt))
                        dst = K[:, mt, nh * 512:(nh + 1) * 512] if kv == 0 else V[:, 0, mt, nh * 512:(nh + 1) * 512]
                        drained(act.copy(dst, b))
            for t in range(NT):
                n = rows(t)
                if t:
                    act.wait_ge(y_done, t)
                b = begin(("tx", t))
                drained(act.copy(XTK[0:n], b[0:n, :].rearrange("p (h q) -> p h q", h=HS)))
                b = begin(("tb", t))
                drained(act.copy(BT[0:n, :], b[0:n, 0:256]))
                wait_drained(act, ("ac", t))
                for g in range(2):
                    b = begin(("ab", t, g)).rearrange("p (h l) -> p h l", h=4)
                    act.copy(E3[:, HS + 4 * g:HS + 4 * g + 4], b[:, :, n - 1])
                    for h in range(4):
                        hh = 4 * g + h
                        last = act.activation(LE[0:n, hh, 0:n], b[0:n, h, 0:n], ACT.Relu, bias=E3[0:n, hh:hh + 1], scale=-1.0)
                    drained(last)
                act.wait_ge(ev["A"], ORD[("ab", t, 1)] + 1)
                act.activation(LE[0:n, :, 0:n], LE[0:n, :, 0:n], ACT.Exp, scale=-1.0).then_inc(le_done, 1)
                act.wait_ge(dec_done, t + 1)
                act.activation(EX[:, :], E3[:, :], ACT.Exp).then_inc(ex_done, 1)
                act.wait_ge(y_done, t + 1)
                root_mean_square(T1[0:n], Y[0:n], n, 8 + t, DSSD)
                if t >= NP - 1:
                    b = begin(("ho", t - NP + 1))
                    drained(act.copy(HO[:, t - NP + 1, :], b))

            def squares(base, need):
                for t in range(NT):
                    n = rows(t)
                    wait_drained(act, need(t))
                    root_mean_square(XN[0:n, t, :], X[0:n, t, :], n, base + t, D)

            squares(13, lambda t: ("o", 1, t))
            for m in range(8):
                b = begin(("q", m, 0))
                drained(act.copy(QT[:, m, halves[0]], b[:, 0:256]))
            for t in range(NT):
                n = rows(t)
                if t >= 2:
                    wait_job(act, ("pt", t - 2, 1))
                for hp in range(2):
                    act.wait_ge(mx_done, 2 * t + hp + 1)
                    b = begin(("s", t, hp))
                    for h in range(2):
                        hh = 2 * hp + h
                        last = act.activation(PR[0:n, t % 2, hh, :], b[0:n, h * NMEM:(h + 1) * NMEM], ACT.Exp,
                                              bias=MX[0:n, (t % 2) * MH + hh:(t % 2) * MH + hh + 1], scale=MD ** -0.5,
                                              accum_out=PS_[0:n, (t % 2) * MH + hh:(t % 2) * MH + hh + 1])
                    drained(last)
                for q in range(2):
                    b = begin(("pt", t, q)).rearrange("p (c m) -> p c m", c=4)
                    drained(act.copy(PT[:, t % 2, 4 * q:4 * q + 4, 0:n], b[:, :, 0:n]))
            squares(18, lambda t: ("mo", 1, t))
            act.wait_ge(outs, 16 * 8)
            for q in range(4):
                b = begin(("sk", q))
                drained(act.copy(SKT[:, 4 * q:4 * q + 4, :], b.rearrange("p (c m) -> p c m", c=4)))
            for t in range(NT):
                for q in range(2):
                    b = begin(("xt", 2, t, q)).rearrange("p (c m) -> p c m", c=4)
                    drained(act.copy(XT[:, 4 * q:4 * q + 4, cx(t)], b[:, :, 0:rows(t)]))
            for m in range(16):
                b = begin(("pq", m, 0))
                drained(act.copy(QP[:, m, halves[0]], b[:, 0:256]))
            for t in range(NT):
                for b4 in (0, 2):
                    b = begin(("sc", t, b4))
                    drained(act.copy(SC[0:rows(t), t, b4 * 512:(b4 + 1) * 512], b[0:rows(t), :]))

            def gates(before):
                act.wait_ge(lg_done, before + 1)
                act.activation(GT[:, :, :], GT[:, :, :], ACT.Exp).then_inc(ge_done, 1)

            def weights(i, par, diag, next_tile=None):
                act.wait_ge(u_used, i * TOPK + TOPK)
                act.activation(GH[:, par, :], HID[:, par, :], ACT.Gelu).then_inc(gelu_done, 1)
                act.wait_ge(w_done, i + 2)
                if next_tile is not None:
                    gates(next_tile)
                for s in range(TOPK):
                    if not (isinstance(i, int) and i * TOPK + s - RD + 1 <= 0):
                        act.wait_ge(v_used, i * TOPK + (s - RD + 1))
                    act.activation(DG[:, s % RD, :], diag, ACT.Copy, scale=WT[:, par, s:s + 1]).then_inc(diag_done, 1)

            def tile_leaves(t, n, before):
                act.wait_ge(v_used, (before + 1) * (PH * TOPK) if n == P else STEPS * TOPK)
                for hf in range(2):
                    dst = X[0:n, t, hf * 512:(hf + 1) * 512] if isinstance(t, int) else X[:, bass.ds(t, 1), hf * 512:(hf + 1) * 512]
                    last = act.copy(dst, PSB[0:n, hf, :] if isinstance(t, int) else PSB[0:n, hf:hf + 1, :])
                last.then_inc(tile_out, 1)

            act.sem_inc(tile_out, 1)
            gates(0)
            weights(0, 0, ident[:, :])
            weights(1, 1, ident[:, :])
            with act.Fori(1, PH // 2 - 1) as j:
                weights(2 * j, 0, ident[:, :])
                weights(2 * j + 1, 1, ident[:, :])
            weights(PH - 2, 0, ident[:, :])
            weights(PH - 1, 1, ident[:, :], next_tile=1)
            tile_leaves(0, P, 0)
            with act.Fori(1, NP) as t:
                with act.Fori(0, PH // 2 - 1) as j:
                    weights(t * PH + 2 * j, 0, ident[:, :])
                    weights(t * PH + 2 * j + 1, 1, ident[:, :])
                weights(t * PH + PH - 2, 0, ident[:, :])
                weights(t * PH + PH - 1, 1, ident[:, :], next_tile=t + 1)
                tile_leaves(t, P, t)
            weights(STEPS - 2, 0, stk[:, :])
            weights(STEPS - 1, 1, stk[:, :])
            tile_leaves(NP, SAM, NP)
            for t in range(NT):
                n = rows(t)
                act.wait_ge(tile_out, t + 2)
                root_mean_square(XN[0:n, t, :], X[0:n, t, :], n, 23 + t, D)

        @block.vector
        def _(dve):
            def begin(key):
                wait_job(dve, key)
                return bank_of(key)

            def drained(ins):
                ins.then_inc(ev["D"], 1)

            nstep = [0]

            def link(ins):
                nstep[0] += 1
                ins.then_inc(dve_step, 1)
                dve.wait_ge(dve_step, nstep[0])

            def inv_rms(col, n, count):
                dve.wait_ge(sq_done, count)
                link(dve.reciprocal(RS[0:n, col:col + 1], SS[0:n, col:col + 1]))

            def scaled_drain(key, dst, col, n, chunks):
                b = begin(key).rearrange("p (c m) -> p c m", c=4)[:, 0:chunks, 0:n]
                drained(dve.tensor_tensor(dst, b, bc(SMT[:, col:col + chunks].unsqueeze(2), [P, chunks, n]), ALU.mult))

            b = begin("sm")
            dve.wait_ge(const_ok, 1)
            dve.tensor_copy(SMT[:, :], b[:, 0:SM_ROWS]).then_inc(ev["D"], 1)
            dve.wait_ge(ev["D"], 1)
            dve.tensor_copy(U[:, :, SEQ + 2:SEQ + 4], SMT[:, SM_HA:SM_HA + 8].rearrange("p (k c) -> p c k", k=2))
            link(dve.tensor_copy(XB[:, :, SEQ + 3:SEQ + 6], SMT[:, SM_HS:SM_HS + 24].rearrange("p (k c) -> p c k", k=3)))
            b = begin("hi")
            drained(dve.tensor_copy(HST[:, 1, :], b))
            dve.memset(HST[:, 0, :], 0.0).then_inc(h_done, 1)
            for t in range(NT):
                n = rows(t)
                inv_rms(t, n, t + 1)
                dve.tensor_scalar(XN[0:n, t, :], X[0:n, t, :], RS[0:n, t:t + 1], None, ALU.mult).then_inc(xs_done, 1)
                for q in range(2):
                    scaled_drain(("xt", 0, t, q), XT[:, 4 * q:4 * q + 4, cx(t)], SM_MIX + 4 * q, n, 4)
            for t in range(2):
                inv_rms(5 + t, P, NT + t + 1)
                dve.tensor_scalar(MEM[:, t, :], MEM[:, t, :], RS[:, 5 + t:6 + t], None, ALU.mult).then_inc(xs_done, 1)
            for t in range(2):
                for q in range(2):
                    scaled_drain(("mt", t, q), MT[:, 4 * q:4 * q + 4, t * P:(t + 1) * P], SM_MEMN + 4 * q, P, 4)
            for m in range(4):
                for hf in range(2):
                    wait_drained(dve, ("in", "gc", m, hf))
                    b = begin(("in", "v", m, hf))
                    for s_, d_ in segs(hf, 2):
                        last = dve.tensor_tensor(U[:, m, d_], b[:, s_], U[:, m, d_], ALU.mult)
                    drained(last)
            wait_drained(dve, ("in", "gb", 3, 1))
            dve.wait_ge(ev["D"], ORD[("in", "v", 3, 1)] + 1)
            for c in range(4):
                w = lambda k: SMT[:, SM_CA + 4 * k + c:SM_CA + 4 * k + c + 1]
                acc = CT[:, c % 2, 0:LG]
                link(dve.tensor_scalar(acc, U[:, c, 0:LG], w(0), None, ALU.mult))
                for k in (1, 2):
                    link(dve.scalar_tensor_tensor(out=acc, in0=U[:, c, k:k + LG], scalar=w(k), in1=acc, op0=ALU.mult, op1=ALU.add))
                dve.tensor_tensor(GB[:, c, :], GB[:, c, :], acc, ALU.mult).then_inc(ya_done, 1)
                dve.wait_ge(ya_done, c + 1)
            for name, base in (("x0", 0), ("x1", 4)):
                for m in (1, 3):
                    for hf in range(2):
                        b = begin(("in", name, m, hf))
                        for s_, d_ in segs(hf, 3):
                            last = dve.tensor_copy(XB[:, base + m, d_], b[:, s_])
                        drained(last)
            b = begin("dt")
            dve.wait_ge(vec_in, 48)
            dve.tensor_tensor(DTV[:, 0, 0:NP * HS].rearrange("p (t h) -> p t h", h=HS), b[:, 0:NP * HS].rearrange("p (t h) -> p t h", h=HS),
                              bc(VB[:, 0:HS].unsqueeze(1), [P, NP, HS]), ALU.add)
            drained(dve.tensor_tensor(DTV[0:SAM, 0, NP * HS:], b[0:SAM, NP * HS:NT * HS], VB[0:SAM, 0:HS], ALU.add))
            dve.wait_ge(ev["D"], ORD["dt"] + 1)
            dve.scalar_tensor_tensor(out=DTV[:, 1, :], in0=DTV[:, 0, :], scalar=-1.0, in1=DTV[:, 0, :], op0=ALU.mult, op1=ALU.min).then_inc(sp_nx, 1)
            dve.wait_ge(sp_e, 1)
            dve.tensor_scalar(DTV[:, 3, :], DTV[:, 2, :], 1.0, None, ALU.add).then_inc(sp_u, 1)
            dve.wait_ge(sp_u, 1)
            link(dve.tensor_scalar(DTV[:, 5, :], DTV[:, 3, :], -1.0, None, ALU.add))
            link(dve.scalar_tensor_tensor(out=DTV[:, 7, :], in0=DTV[:, 5, :], scalar=0.0, in1=DTV[:, 2, :], op0=ALU.is_equal, op1=ALU.mult))
            dve.wait_ge(sp_l, 1)
            link(dve.scalar_tensor_tensor(out=DTV[:, 4, :], in0=DTV[:, 5, :], scalar=0.0, in1=DTV[:, 4, :], op0=ALU.not_equal, op1=ALU.mult))
            link(dve.tensor_scalar(DTV[:, 5, :], DTV[:, 5, :], 2.0 ** -24, None, ALU.max))
            link(dve.reciprocal(DTV[:, 5, :], DTV[:, 5, :]))
            link(dve.tensor_tensor(DTV[:, 4, :], DTV[:, 4, :], DTV[:, 2, :], ALU.mult))
            link(dve.tensor_tensor(DTV[:, 4, :], DTV[:, 4, :], DTV[:, 5, :], ALU.mult))
            link(dve.tensor_tensor(DTV[:, 4, :], DTV[:, 4, :], DTV[:, 7, :], ALU.add))
            link(dve.scalar_tensor_tensor(out=DTV[:, 6, :], in0=DTV[:, 0, :], scalar=0.0, in1=DTV[:, 4, :], op0=ALU.max, op1=ALU.add))
            dve.wait_ge(ea_done, 1)
            v3 = lambda r: DTV[:, r, :].rearrange("p (t h) -> p t h", h=HS)
            dve.scalar_tensor_tensor(out=v3(7), in0=v3(6), scalar=-1.0, in1=bc(EA[:, :].unsqueeze(1), [P, NT, HS]),
                                     op0=ALU.mult, op1=ALU.mult).then_inc(dta_done, 1)
            dve.wait_ge(dta_done, 1)
            wait_drained(dve, ("in", "x1", 2, 1))
            dve.wait_ge(ev["D"], ORD[("in", "x1", 3, 1)] + 1)
            for j, c0, nk, ln in ((0, SEQ, 2, U), (8, SEQ + SAM + 2, 2, U), (16, SEQ, 3, XB), (40, SEQ + SAM + 3, 3, XB)):
                nch = 4 if nk == 2 else 8
                last = dve.tensor_copy(OC[:, j:j + nk * nch].rearrange("p (k c) -> p c k", k=nk), ln[:, :, c0:c0 + nk])
            last.then_inc(oc_done, 1)
            dve.wait_ge(oc_done, 1)
            for c in range(8):
                w = lambda k: SMT[:, SM_CS + 8 * k + c:SM_CS + 8 * k + c + 1]
                if c >= 2:
                    dve.wait_ge(silu_done, c - 1)
                if c == 0:
                    dve.wait_ge(ev["D"], ORD["dt"] + 1)
                acc = CT[:, c % 2, 0:LX - 3]
                link(dve.tensor_scalar(acc, XB[:, c, 0:LX - 3], w(0), None, ALU.mult))
                for k in (1, 2):
                    link(dve.scalar_tensor_tensor(out=acc, in0=XB[:, c, k:k + LX - 3], scalar=w(k), in1=acc, op0=ALU.mult, op1=ALU.add))
                dve.scalar_tensor_tensor(out=acc, in0=XB[:, c, 3:LX], scalar=w(3), in1=acc, op0=ALU.mult, op1=ALU.add).then_inc(conv_done, 1)
            b = begin("oc")
            drained(dve.tensor_copy(OCT[:, :], b[0:64, 0:P]))
            for st in range(2):
                for q in range(4):
                    b = begin(("kt", st, q)).rearrange("p (c m) -> p c m", c=2)
                    drained(dve.tensor_copy(KT[:, st, 2 * q:2 * q + 2, :], b))

            for t in range(NT):
                n, k = rows(t), int(t == NP)
                dt_b = bc(DTV[0:n, 6, t * HS:(t + 1) * HS].unsqueeze(2), [n, HS, HP])
                dve.tensor_copy(DA[0:n], bc(DTV[0:n, 7, t * HS:(t + 1) * HS].unsqueeze(2), [n, HS, P])).then_inc(da_done, 1)
                b = begin(("ac", t))
                drained(dve.tensor_copy(E3[0:n, 0:HS], b[0:n, 0:HS]))
                b = begin(("cb", t)).rearrange("p (g l) -> p g l", g=4)
                drained(dve.tensor_tensor(CBM[0:n, :, 0:n], b[0:n, 0:2, 0:n], bc(tri[0:n, 0:n].unsqueeze(1), [n, 2, n]), ALU.mult))
                wait_drained(dve, ("tx", t))
                dve.tensor_tensor(XDT[0:n], XTK[0:n], dt_b, ALU.mult).then_inc(xdt_done, 1)
                wait_drained(dve, ("ab", t, 1))
                dve.wait_ge(ev["D"], ORD[("cb", t)] + 1)
                dve.tensor_tensor(E3[0:n, 2 * HS:], E3[0:n, HS:2 * HS], E3[0:n, 0:HS], ALU.subtract).then_inc(dec_done, 1)
                dve.wait_ge(le_done, t + 1)
                for g in range(2):
                    last = dve.tensor_tensor(LE[0:n, 4 * g:4 * g + 4, 0:n], LE[0:n, 4 * g:4 * g + 4, 0:n],
                                             bc(CBM[0:n, g:g + 1, 0:n], [n, 4, n]), ALU.mult)
                last.then_inc(m_done, 1)
                dve.wait_ge(ex_done, t + 1)
                dve.wait_ge(xdt_done, t + 1)
                dve.tensor_tensor(XDD[0:n], XDT[0:n], bc(EX[0:n, 2 * HS:].unsqueeze(2), [n, HS, HP]), ALU.mult).then_inc(xdd_done, 1)
                b = begin(("yo", t)).rearrange("p (h q) -> p h q", h=HS)
                dve.tensor_tensor(T1[0:n], b[0:n], bc(EX[0:n, 0:HS].unsqueeze(2), [n, HS, HP]), ALU.mult).then_inc(ev["D"], 1)
                hst = HST[:, k, :].rearrange("p (h q) -> p h q", h=HS)
                link(dve.tensor_tensor(hst, hst, bc(EX[:, HS:2 * HS].unsqueeze(2), [P, HS, HP]), ALU.mult))
                b = begin(("yd", t)).rearrange("p (h q) -> p h q", h=HS)
                dve.tensor_tensor(T1[0:n], T1[0:n], b[0:n], ALU.add).then_inc(ev["D"], 1)
                if t:
                    wait_job(dve, ("yt", t - 1))
                link(dve.tensor_tensor(Y[0:n], XTK[0:n], bc(VB[0:n, 2 * HS:].unsqueeze(2), [n, HS, HP]), ALU.mult))
                b = begin(("st", t))
                dve.tensor_tensor(HST[:, k, :], HST[:, k, :], b, ALU.add).then_inc(ev["D"], 1)
                dve.wait_ge(ev["D"], ORD[("st", t)] + 1)
                link(dve.tensor_tensor(Y[0:n], Y[0:n], T1[0:n], ALU.add))
                dve.tensor_tensor(Y[0:n], Y[0:n], ZS[0:n, t, :].rearrange("p (h q) -> p h q", h=HS), ALU.mult).then_inc(y_done, 1)
                inv_rms(8 + t, n, NT + 2 + t + 1)
                dve.wait_ge(y_done, t + 1)
                dve.tensor_scalar(Y[0:n], Y[0:n], RS[0:n, 8 + t:9 + t], None, ALU.mult).then_inc(xs_done, 1)
                scaled_drain(("yt", t), YBT[:, :, cx(t)], SM_SSD, n, 4)

            def residual(kind):
                for nh in range(2):
                    for t in range(NT):
                        n = rows(t)
                        b = begin((kind, nh, t))
                        xs = X[0:n, t, nh * 512:(nh + 1) * 512]
                        drained(dve.tensor_tensor(xs, b[0:n, :], xs, ALU.add))

            residual("o")
            for t in range(NT):
                n = rows(t)
                inv_rms(13 + t, n, 2 * NT + 2 + t + 1)
                dve.tensor_scalar(XN[0:n, t, :], X[0:n, t, :], RS[0:n, 13 + t:14 + t], None, ALU.mult).then_inc(xs_done, 1)
                for q in range(2):
                    scaled_drain(("xt", 1, t, q), XT[:, 4 * q:4 * q + 4, cx(t)], SM_LMEM + 4 * q, n, 4)
            for m in range(8):
                b = begin(("q", m, 1))
                drained(dve.tensor_copy(QT[:, m, halves[1]], b[:, 0:288]))
            for t in range(NT):
                n, o4 = rows(t), (t % 2) * MH
                for hp in range(2):
                    b = begin(("s", t, hp)).rearrange("p (h m) -> p h m", h=2)
                    mx = MX[0:n, o4 + 2 * hp:o4 + 2 * hp + 2]
                    link(dve.tensor_reduce(mx, b[0:n], AXX, ALU.max))
                    dve.tensor_scalar(mx, mx, -MD ** -0.5, None, ALU.mult).then_inc(mx_done, 1)
                wait_drained(dve, ("s", t, 1))
                rc = PS_[0:n, 2 * MH + o4:2 * MH + o4 + MH]
                link(dve.reciprocal(rc, PS_[0:n, o4:o4 + MH]))
                dve.tensor_tensor(PR[0:n, t % 2], PR[0:n, t % 2], bc(rc.unsqueeze(2), [n, MH, NMEM]), ALU.mult).then_inc(p_done, 1)
                for q in range(2):
                    b = begin(("ot", t, q)).rearrange("p (c m) -> p c m", c=4)
                    drained(dve.tensor_copy(QT[:, 4 * q:4 * q + 4, cx(t)], b[:, :, 0:n]))
            residual("mo")
            dve.wait_ge(gffn_in, 32)
            for t in range(NT):
                n = rows(t)
                inv_rms(18 + t, n, 3 * NT + 2 + t + 1)
                dve.scalar_tensor_tensor(out=XN[0:n, t, :], in0=X[0:n, t, :], scalar=RS[0:n, 18 + t:19 + t], in1=GB_FFN[0:n, :],
                                         op0=ALU.mult, op1=ALU.mult).then_inc(xs_done, 1)
            for m in range(16):
                b = begin(("pq", m, 1))
                drained(dve.tensor_copy(QP[:, m, halves[1]], b[:, 0:288]))
            wait_job(dve, ("pq", 15, 1))
            link(dve.memset(SC[:, NP, :], 0.0))
            for t in range(NT):
                for b4 in (1, 3):
                    b = begin(("sc", t, b4))
                    drained(dve.tensor_copy(SC[0:rows(t), t, b4 * 512:(b4 + 1) * 512], b[0:rows(t), :]))

            TK = [0]

            def topk(i, head):
                base = i * TOPK_LINKS
                k = [0]

                def link(ins):
                    k[0] += 1
                    ins.then_inc(topk_step, 1)
                    dve.wait_ge(topk_step, base + k[0])

                def also(ins):
                    k[0] += 1
                    ins.then_inc(topk_step, 1)

                def sync():
                    dve.wait_ge(topk_step, base + k[0])
                    dve.sem_inc(dve_passed, 1)

                also(dve.tensor_copy(TS[:, :, :].rearrange("p a b -> p (a b)"),
                                     SC[:, :, :].rearrange("p t k -> p (t k)")[:, bass.ds(i * 256, 256)]))
                sync()
                for h in range(2):
                    also(dve.max(TV[:, h, 0:8], TS[:, h, :]))
                sync()
                for h in range(2):
                    also(dve.max_index(TI[:, h, 0:8], TV[:, h, 0:8], TS[:, h, :]))
                    also(dve.match_replace(TS2[:, h, :], TV[:, h, 0:8], TS[:, h, :], NEG))
                sync()
                for h in range(2):
                    also(dve.max(TV[:, h, 8:16], TS2[:, h, :]))
                sync()
                for h in range(2):
                    also(dve.max_index(TI[:, h, 8:16], TV[:, h, 8:16], TS2[:, h, :]))
                also(dve.tensor_tensor(CO, bc(TV[:, 0, :].unsqueeze(2), [P, TOPK, TOPK]), bc(TV[:, 1:2, :], [P, TOPK, TOPK]), ALU.add))
                sync()
                also(dve.max(CV[:, 0:8], COF))
                sync()
                also(dve.max_index(CP[:, 0:8], CV[:, 0:8], COF))
                also(dve.match_replace(CO2, CV[:, 0:8], COF, NEG))
                sync()
                also(dve.max(CV[:, 8:16], CO2))
                sync()
                link(dve.max_index(CP[:, 8:16], CV[:, 8:16], CO2))
                also(dve.tensor_copy(TL.rearrange("p h k -> p (h k)")[:, bass.ds(head * TOPK, TOPK)], CV))
                also(dve.tensor_scalar(CA[:, 0, :], CP, 4, None, ALU.logical_shift_right))
                link(dve.tensor_scalar(CA[:, 1, :], CP, 15, None, ALU.bitwise_and))
                e3 = [EQ[:, h, :].rearrange("p (k j) -> p k j", j=TOPK) for h in range(2)]
                for h in range(2):
                    also(dve.tensor_tensor(e3[h], bc(CA[:, h, :].unsqueeze(2), [P, TOPK, TOPK]),
                                           bc(iota[:, :].unsqueeze(1), [P, TOPK, TOPK]), ALU.is_equal))
                dve.wait_ge(topk_step, base + k[0])
                for h in range(2):
                    also(dve.tensor_tensor(e3[h], e3[h], bc(TI[:, h:h + 1, :], [P, TOPK, TOPK]), ALU.mult))
                dve.wait_ge(topk_step, base + k[0])
                link(dve.tensor_reduce(EQS, EQ.rearrange("p h (k j) -> p h k j", j=TOPK), AXX, ALU.add))
                dve.scalar_tensor_tensor(out=IDX[:, bass.ds(i * TOPK, TOPK)], in0=EQS[:, 0, :], scalar=float(NK),
                                         in1=EQS[:, 1, :], op0=ALU.mult, op1=ALU.add).then_inc(topk_done, 1)
                assert k[0] == TOPK_LINKS, k[0]

            TOPK_LINKS = 25

            def gates(before):
                dve.wait_ge(topk_done, (before + 1) * PH)
                dve.wait_ge(w_done, before * PH + 1)
                dve.tensor_tensor(GT, TL, bc(TL[:, :, 0:1], [P, PH, TOPK]), ALU.subtract).then_inc(lg_done, 1)
                dve.wait_ge(ge_done, before + 1)
                dve.tensor_reduce(GS[:, 0, :], GT, AXX, ALU.add).then_inc(gate_step, 1)
                dve.wait_ge(gate_step, 2 * before + 1)
                dve.reciprocal(GS[:, 1, :], GS[:, 0, :]).then_inc(gate_step, 1)
                dve.wait_ge(gate_step, 2 * before + 2)
                dve.tensor_tensor(GT, GT, bc(GS[:, 1, :].unsqueeze(2), [P, PH, TOPK]), ALU.mult).then_inc(gate_done, 1)
                dve.wait_ge(gate_done, before + 1)

            def dots(i, par):
                for s in range(TOPK):
                    dve.wait_ge(u_in[s % RU], i * (16 * TOPK // RU) + 16 * (s // RU + 1))
                    u = UR[:, s % RU, :]
                    dve.tensor_tensor_reduce(u, u, XNB, 1.0, 0.0, ALU.mult, ALU.add, HID[:, par, s:s + 1]).then_inc(u_used, 1)

            def gated(i, par, head):
                dve.wait_ge(gelu_done, i + 1)
                dve.tensor_tensor(WT[:, par, :], GH[:, par, :],
                                  GTF[:, head * TOPK:(head + 1) * TOPK] if isinstance(head, int) else GTF[:, bass.ds(head * TOPK, TOPK)],
                                  ALU.mult).then_inc(w_done, 1)

            dve.wait_ge(ev["A"], TOTAL["A"])
            dve.wait_ge(ev["D"], TOTAL["D"])
            dve.sem_inc(w_done, 1)
            with dve.Fori(0, PH) as h:
                topk(h, h)
            with dve.Fori(0, NP) as t:
                gates(t)
                dve.tensor_copy(XNB, XNt[:, bass.ds(t * D, D)]).then_inc(xnb_done, 1)
                dve.wait_ge(xnb_done, t + 1)
                dve.sem_inc(dve_passed, 1)
                with dve.Fori(0, PH // 2) as j:
                    for par in range(2):
                        dots(t * PH + 2 * j + par, par)
                        topk((t + 1) * PH + 2 * j + par, 2 * j + par)
                        gated(t * PH + 2 * j + par, par, 2 * j + par)
            gates(NP)
            dve.wait_ge(relaid_g, 96)
            dve.tensor_copy(XNB, XN[:, NP, :]).then_inc(xnb_done, 1)
            dve.wait_ge(xnb_done, NP + 1)
            for par in range(2):
                dots(STEPS - 2 + par, par)
                gated(STEPS - 2 + par, par, par)
            for t in range(NT):
                n = rows(t)
                inv_rms(23 + t, n, 4 * NT + 2 + t + 1)
                dve.scalar_tensor_tensor(out=XN[0:n, t, :], in0=X[0:n, t, :], scalar=RS[0:n, 23 + t:24 + t], in1=GB_FIN[0:n, :],
                                         op0=ALU.mult, op1=ALU.mult).then_inc(y_norm, 1)


_INS = ["x_prompt", "x_sample", "mem_prompt", "cache_conv_a", "cache_conv_ssd", "state_ssd", "cache_mem_k", "cache_mem_v",
        "ln_mix_w", "w_in", "conv_a_w", "conv_s_w", "conv_s_b", "dt_bias", "a_log", "d_skip", "ssd_norm_w", "w_out",
        "ln_mem_w", "mem_norm_w", "w_mq", "w_mk", "w_mv", "w_mo", "ln_ffn_w", "w_pq", "sub_keys", "u_tab", "v_tab",
        "final_norm_w"]
_OUTS = [("y_prompt", (1, 512, 1024)), ("y_sample", (1, 32, 1024)), ("ca_p", (1, 1, 2, 512)), ("cs_p", (1, 1, 3, 1024)),
         ("st_p", (1, 1, 8, 64, 128)), ("mk", (1, 1, 256, 4, 256)), ("mv", (1, 1, 256, 4, 256)),
         ("ca_s", (1, 1, 2, 512)), ("cs_s", (1, 1, 3, 1024)), ("st_s", (1, 1, 8, 64, 128))]


def kernel(**inputs):
    import numpy as _np
    import concourse.bacc as _bacc
    from concourse import mybir as _mybir
    from concourse.bass_utils import run_bass_kernel_spmd as _run

    nc = _bacc.Bacc("TRN2", target_bir_lowering=False, num_devices=1)
    arrays, ins, outs = {}, {}, {}
    for name in _INS:
        arr = _np.ascontiguousarray(inputs[name])
        arrays[f"in_{name}"] = arr
        ins[name] = nc.dram_tensor(f"in_{name}", arr.shape, _mybir.dt.from_np(arr.dtype), kind="ExternalInput").ap()
    for name, shape in _OUTS:
        outs[name] = nc.dram_tensor(f"out_{name}", shape, _mybir.dt.float32, kind="ExternalOutput").ap()
    build_program(nc, ins, outs)
    r = _run(nc, [arrays], core_ids=[0])
    return tuple(r.results[0][f"out_{name}"] for name, _ in _OUTS)
```

```python
from contextlib import ExitStack

import numpy as np
import concourse.bass as bass
from concourse import mybir

ALU = mybir.AluOpType
ACT = mybir.ActivationFunctionType
AXX = mybir.AxisListType.X
F32 = mybir.dt.float32
U32 = mybir.dt.uint32

P = 128
D = 1024
DC = D // P
SEQ, SAM = 512, 32
NT = 5
NP = SEQ // P
DCONV, DSSD, XBC = 512, 512, 1024
HS, HP, NS = 8, 64, 128
NMEM, MH, MD = 256, 4, 256
PH, NK, TOPK = 8, 128, 16
EPS = 1e-6
NEG = -3.0e38
NB = 6
BW = 256
NW = 3
RA, RB = 4, 8
RD = 4
VE = 1
STEPS = NP * PH + 2

SM_MIX, SM_MEMN, SM_LMEM, SM_SSD, SM_CA, SM_CS, SM_CB, SM_HA, SM_HS = 0, 8, 16, 24, 28, 40, 72, 80, 88
SM_ROWS = 112


TG = [[0, 1], [2, 3, 4]]
NG = [2 * P, 2 * P + SAM]
QP4 = TOPK // 4
A_STEPS = 2 * PH
SHARED = A_STEPS - 1


def rows(t):
    return P if t < NP else SAM


def group(t):
    return int(t >= 2)


def dense(g):
    s = []
    if g == 0:
        s += [("const",)]
        for t in TG[0]:
            s += [("norm", 0, t), ("turn", 0, t)]
    else:
        s += [("turn", 0, t) for t in TG[1]]
    for b in ("gc", "v", "gb", "x0"):
        s += [("in", g, b, m) for m in range(4)]
        if g == 0 and b in ("gc", "v"):
            s += [("memn", "gc v".split().index(b))]
    s += [("keep", g, "u"), ("keep", g, "x0")]
    s += [("ca", g, 0), ("ca", g, 1), ("in", g, "x1", 0), ("ca", g, 2), ("in", g, "x1", 1), ("ca", g, 3), ("cs", g, 0),
          ("in", g, "x1", 2), ("cs", g, 1), ("in", g, "x1", 3), ("dt", g), ("keep", g, "x1"), ("cs", g, 2)]
    z = [("z", g, q, t) for q in range(2) for t in TG[g]]
    for c in range(3, 8):
        s += z[:1] + [("cs", g, c)]
        z = z[1:]
    s += z
    kv = [("kv", kv, q, mt) for kv in range(2) for q in range(4) for mt in range(2)] if g == 0 else [("oc",)]
    for t in TG[g]:
        for part in ("s1", "s2", "s3", "s4"):
            s += [(part, t)] + kv[:2]
            kv = kv[2:]
        if t >= NP - 1:
            s += [("ho", t - NP + 1)]
    s += kv
    s += [("o", g, q, t) for q in range(4) for t in TG[g]]
    s += [("norm", 1, t) for t in TG[g]]
    if g == 0:
        s += [("kt", 0, 0, q) for q in range(4)]
    s += [("turn", 1, t) for t in TG[g]]
    if g == 1:
        s += [("kt", 1, st, q) for st in range(2) for q in range(4)]
    s += [("q", g, m) for m in range(8)]
    for i, t in enumerate(TG[g]):
        s += [("a1", t)] + ([("a2", TG[g][i - 1])] if i else [])
    s += [("a2", TG[g][-1])]
    s += [("mo", g, q, t) for q in range(4) for t in TG[g]]
    s += [("norm", 2, t) for t in TG[g]] + [("sk", g, q) for q in range(4)] + [("turn", 2, t) for t in TG[g]]
    if g == 1:
        s += [("pq", g, m) for m in range(16)]
        s += [("sc", t, b) for t in TG[g] for b in range(4)]
        return s
    s += [("norm", 0, t) for t in TG[1]]
    for m in range(16):
        s += [("pq", 0, m)]
        if m % 4 == 0 and m:
            s += [("sc", 0, m // 4 - 1)] + [("start",)] * (m == 4)
        if m in (5, 8, 12, 15):
            s += [("g", 0, (5, 8, 12, 15).index(m))]
    s += [("sc", 0, 3)] + [("sc", 1, b) for b in range(4)]
    return s


COST = {"norm": 0.5, "turn": 1.6, "in": 3.8, "q": 3.8, "pq": 3.8, "z": 3.4, "o": 3.4, "mo": 3.4, "s1": 5, "s2": 6, "s3": 7, "s4": 3,
        "a1": 7, "a2": 8, "sc": 0.9, "kt": 0.4, "sk": 0.4, "ca": 1.5, "cs": 2}


def mix():
    gather = [("r", 0)] + [x for i in range(1, A_STEPS) for x in [("g", i, k) for k in range(4)] + [("r", i)]]
    gather.insert(gather.index(("r", PH)) + 1, ("leave", 0))
    gather.insert(gather.index(("r", PH + 1)) + 1, ("final", 0))
    slots = [x for x in gather if x[0] == "g" and x[1] < A_STEPS - 2]
    work, out, spent, k = dense(1), [], 0.0, 0
    total = sum(COST.get(w[0], 0.5) for w in work)
    for x in gather:
        out.append(x)
        if x[0] == "r" and x[1] < A_STEPS - 2 or x in slots and x[2] < 3:
            k += 1
            while work and (spent < total * k / (len(slots) + 1) or (out[-1][0] == "a1" and work[0][0] == "a2")):
                spent += COST.get(work[0][0], 0.5)
                out.append(work.pop(0))
    return out + work


DENSE0, MIX = dense(0), mix()


def jobs_of(seg):
    k = seg[0]
    if k == "const":
        return [("sm", "D"), ("hi", "D")]
    if k == "turn":
        return [(("xt", seg[1], seg[2], q), "A" if seg[1] == 2 else "D") for q in range(2)]
    if k == "memn":
        return [(("mt", seg[1], q), "D") for q in range(2)]
    if k == "in":
        _, g, b, m = seg
        return [(seg, "D" if b == "v" or (g == 0 and b[0] == "x" and m % 2) else "A")]
    if k in ("z", "kv", "q", "sk", "pq", "ho"):
        return [(seg, "A")]
    if k == "kt":
        return [(seg, "A" if seg[1] else "D")]
    if k == "sc":
        return [(seg, "A")]
    if k in ("dt", "o", "mo", "oc"):
        return [(seg, "D")]
    if k == "s1":
        return [(("tx", seg[1]), "A"), (("tb", seg[1]), "A"), (("ac", seg[1]), "D"), (("cb", seg[1]), "D")]
    if k == "s2":
        return [(("ab", seg[1], 0), "A"), (("ab", seg[1], 1), "A")]
    if k == "s3":
        return [(("yo", seg[1]), "D"), (("yd", seg[1]), "D"), (("st", seg[1]), "D")]
    if k == "s4":
        return [(("yt", seg[1]), "D")]
    if k == "a1":
        return [(("s", seg[1], hp), "A") for hp in range(2)]
    if k == "a2":
        return [(("pt", seg[1], q), "A") for q in range(2)] + [(("ot", seg[1], q), "A") for q in range(2)]
    return []


JOBS = [j for seg in DENSE0 + MIX for j in jobs_of(seg)]
SEQN = {k: n for n, (k, _) in enumerate(JOBS)}
OWNER = dict(JOBS)
ORD = {}
for _own in "AD":
    for _i, _k in enumerate(k for k, o in JOBS if o == _own):
        ORD[_k] = _i
ROOTS = [s for s in DENSE0 + MIX if s[0] in ("norm", "memn", "s4", "leave")] + [("leave", t) for t in range(1, NT)]
SCALED = [s for s in ROOTS if s[0] != "leave"]

BLOCKS = []
for _g in range(2):
    _l = TG[_g][-1]
    BLOCKS += [("w_in", c + BW * h, ("in", _g, b, 2 * h + 1))
               for b, c in (("gc", 512), ("v", 1024), ("gb", 0), ("x0", 2048), ("x1", 2560)) for h in range(2)]
    BLOCKS += [("w_in", 1536 + BW * q, ("z", _g, q, _l)) for q in range(2)]
    if _g == 0:
        BLOCKS += [(w, BW * q, ("kv", kv, q, 1)) for kv, w in enumerate(("w_mk", "w_mv")) for q in range(4)]
    BLOCKS += [("w_out", BW * q, ("o", _g, q, _l)) for q in range(4)]
    BLOCKS += [("w_mq", BW * q, ("q", _g, 2 * q + 1)) for q in range(4)]
    BLOCKS += [("w_mo", BW * q, ("mo", _g, q, _l)) for q in range(4)]
    BLOCKS += [("w_pq", BW * q, ("pq", _g, 2 * q + 1)) for q in range(8)]

def pe_row(i, s):
    if isinstance(i, int) and i < SHARED:
        return i * (TOPK - QP4 * VE) + s // RA * (RA - VE) + s % RA
    return i * TOPK + (s - SHARED * QP4 * VE)


def dve_row(i, s):
    return i * QP4 * VE + s // RA * VE + s % RA - (RA - VE)


def on_dve(i, s):
    return isinstance(i, int) and i < SHARED and s % RA >= RA - VE


BLOCK_AT = {b: i for i, b in enumerate((w, c, k[1] if k[0] != "kv" else 0) for w, c, k in BLOCKS)}
TOPK_LINKS = 24


def build_program(nc, a, o):
    ctx = ExitStack()
    with ctx:
        def sb(name, shape, dt=F32):
            return ctx.enter_context(nc.sbuf_tensor(name, shape, dt))

        def sem(name):
            return ctx.enter_context(nc.semaphore(name))

        X = sb("X", [P, NT, D])
        XN = sb("XN", [P, NT, D])
        ident = sb("ident", [P, P])
        tri = sb("tri", [P, P])
        stk = sb("stk", [P, P])
        EPSC = sb("EPSC", [P, 1])
        iota_i = sb("iota_i", [P, TOPK], mybir.dt.int32)
        iota = sb("iota", [P, TOPK])
        SMR = sb("SMR", [SM_ROWS, P])
        SMT = sb("SMT", [P, SM_ROWS])
        G_FFN = sb("G_FFN", [P, D])
        G_FIN = sb("G_FIN", [P, D])
        VB = sb("VB", [P, 3 * HS])
        IDX = sb("IDX", [P, NT * P], U32)
        OC = sb("OC", [P, 64])
        OCT = sb("OCT", [64, P])
        HU = sb("HU", [P, 4, 2])
        HX = sb("HX", [P, 8, 3])
        DTV = sb("DTV", [P, 8, 3 * HS])
        WDT = sb("WDT", [P, DC, HS])
        E3 = sb("E3", [P, 3 * HS])
        EX = sb("EX", [P, 3 * HS])
        EA = sb("EA", [P, HS])
        SS = sb("SS", [P, 32])
        RS = sb("RS", [P, 32])
        MX = sb("MX", [P, 2 * MH])
        PSM = sb("PSM", [P, 4 * MH])
        HST = sb("HST", [P, 2, 512])
        BIG = sb("BIG", [P, 3 * DC * BW + 4096 + 2 * RA * D])
        PT_ = sb("PEER", [P, 2700])
        AR = sb("AR", [P, 15816])
        PSB = ctx.enter_context(nc.psum_tensor("PSB", [P, 8, 512], F32))

        def cut(mem, off, *shape):
            n = int(np.prod(shape))
            v = mem[:, off:off + n]
            if len(shape) == 2:
                v = v.rearrange("p (a b) -> p a b", a=shape[0])
            if len(shape) == 3:
                v = v.rearrange("p (a b c) -> p a b c", a=shape[0], b=shape[1])
            return v

        WB = cut(BIG, 0, NW, DC, BW)
        SCA = cut(BIG, 6144, 2, 2 * PH * NK)
        ring_a = cut(BIG, 10240, 2 * RA, D)
        UA, VA = ring_a[:, 0:RA], ring_a[:, RA:2 * RA]
        UB, VB_ = cut(BIG, 0, RB, D), ring_a
        LU, LG, LX = [2 + 256, 2 + 256 + 2 + SAM], [256, 256 + 2 + SAM], [3 + 256, 3 + 256 + 3 + SAM]
        XTg = [cut(AR, 0, DC, n) for n in NG]
        U = cut(AR, 2304, 4, LU[1])
        GB = cut(AR, 3472, 4, LG[1])
        XB = cut(AR, 4632, 8, LX[1])
        YBT = cut(AR, 6984, 4, NG[1])
        ZS = cut(AR, 8136, 3, 512)
        XTK = cut(AR, 9672, HS, HP)
        CT = cut(AR, 9672, 2, LX[1])
        XDT = cut(AR, 10184, HS, HP)
        XDD = cut(AR, 10696, HS, HP)
        BT = cut(AR, 11208, 256)
        CBM = cut(AR, 11464, 2, P)
        Y = cut(AR, 11720, HS, HP)
        T1 = cut(AR, 12232, HS, HP)
        DA = cut(AR, 12744, HS, P)
        LE = cut(AR, 13768, HS, P)
        HO = cut(AR, 14792, 2, 512)
        V0 = cut(BIG, 10240, 2, D)
        MEM = V0
        K0 = cut(BIG, 12288, 2, D)
        S0 = cut(BIG, 12288, 4, P)
        MT = cut(BIG, 14336, DC, NMEM)
        KT0 = cut(BIG, 6144, DC, NMEM)
        PR = cut(AR, 0, MH, NMEM)
        PT = cut(AR, 1024, 8, P)
        QTg = [cut(AR, 2304, DC, n) for n in NG]
        KB = [cut(AR, 2304, 2, D), cut(AR, 4608, 2, D)]
        VV = cut(AR, 6656, 2, 2, D)
        KTB = cut(AR, 10752, 2, DC, NMEM)
        QPg = [cut(AR, 2304, 16, n) for n in NG]
        SKT = cut(AR, 6912, 16, P)
        SK = cut(AR, 8960, 16, P)
        SCB = cut(AR, 8960, 3, 2 * PH * NK)
        g_ = [0]

        def take_(*shape, u=False):
            n = int(np.prod(shape))
            v = PT_[:, g_[0]:g_[0] + n]
            g_[0] += n
            if u:
                v = v.bitcast(U32)
            if len(shape) == 2:
                v = v.rearrange("p (a b) -> p a b", a=shape[0])
            return v

        DG = take_(RD, P)
        TS, TS2 = take_(2, P), take_(2, P)
        TV, TI = take_(2, TOPK), take_(2, TOPK, u=True)
        COF = take_(256)
        CO = COF.rearrange("p (a b) -> p a b", a=TOPK)
        CO2 = take_(256)
        CV, CP = take_(TOPK), take_(TOPK, u=True)
        CA = take_(2, TOPK, u=True)
        EQ, EQS = take_(2, TOPK * TOPK), take_(2, TOPK)
        LGS = take_(PH, TOPK)
        LGF = LGS.rearrange("p h k -> p (h k)")
        GS = take_(2, PH)
        GE, GSUM, GR = take_(2, TOPK), take_(2), take_(2)
        HID, GH, WT = take_(2, TOPK), take_(2, TOPK), take_(2, TOPK)
        IU, IV = take_(2, TOPK, u=True), take_(2, TOPK, u=True)
        assert g_[0] <= 2700, g_[0]

        x_in = [sem(f"x_in{t}") for t in range(NT)]
        small_in, vec_in, mem_in, state_in, wdt_in = map(sem, "small_in vec_in mem_in state_in wdt_in".split())
        kv_in, sk_in, gain_in = map(sem, "kv_in sk_in gain_in".split())
        w_in = [sem(f"w_in{i}") for i in range(NW)]
        const_step, const_ok = sem("const_step"), sem("const_ok")
        pe_done = sem("pe_done")
        ev = {"A": sem("act_drained"), "D": sem("dve_drained")}
        act_step, dve_step = sem("act_step"), sem("dve_step")
        root_done = sem("root_done")
        xs_done = sem("xs_done")
        conv_done, silu_done, kept = sem("conv_done"), sem("silu_done"), sem("kept")
        oc_done, outs = sem("oc_done"), sem("outs")
        sp_nx, sp_e, sp_u, sp_l, ea_done, dta_done = map(sem, "sp_nx sp_e sp_u sp_l ea_done dta_done".split())
        da_done, dec_done, ex_done, le_done, m_done, xdt_done, xdd_done, h_done, y_done = map(
            sem, "da_done dec_done ex_done le_done m_done xdt_done xdd_done h_done y_done".split())
        ya_done, mx_done, p_done = map(sem, "ya_done mx_done p_done".split())
        topk_step, topk_done, topk_s_done, lg_done, exp_done, gr_done = map(
            sem, "topk_step topk_done topk_s_done lg_done exp_done gr_done".split())
        lgs_done, exps_done, gates_step, gates_done, sc_clear = map(
            sem, "lgs_done exps_done gates_step gates_done sc_clear".split())
        idx_copied, relaid_x, relaid_i, relaid_g = map(sem, "idx_copied relaid_x relaid_i relaid_g".split())
        ua_in, va_in = [sem(f"ua_in{r}") for r in range(RA)], [sem(f"va_in{r}") for r in range(RA)]
        ub_in, vb_in = [sem(f"ub_in{r}") for r in range(RB)], [sem(f"vb_in{r}") for r in range(RB)]
        u_used, v_used, v_added, gelu_done, w_done, diag_done, tile_closed, tile_out = map(
            sem, "u_used v_used v_added gelu_done w_done diag_done tile_closed tile_out".split())
        y_norm, y_out = sem("y_norm"), sem("y_out")
        dve_passed, pool_passed = sem("dve_passed"), sem("pool_passed")

        def loc(t, gap=0):
            s0 = (t - TG[group(t)][0]) * P
            return slice(s0 + (gap if t == NP else 0), s0 + (gap if t == NP else 0) + rows(t))

        def segs(g, hist):
            first = (slice(0, 256), slice(hist, hist + 256))
            if g == 0:
                return [first]
            s0 = 256 + {0: 2, 2: 4, 3: 6}[hist]
            return [first, (slice(256, 256 + SAM), slice(s0, s0 + SAM))]

        def wait_job(eng, key):
            eng.wait_ge(pe_done, SEQN[key] + 1)

        def wait_drained(eng, key):
            eng.wait_ge(ev[OWNER[key]], ORD[key] + 1)

        def bank_of(key):
            return PSB[:, 2 + SEQN[key] % NB, :]

        def bc(ap, shape):
            return ap.broadcast_to(shape)

        def u_row(i, s):
            return UA[:, s % RA, :] if isinstance(i, int) and i < A_STEPS else UB[:, s % RB, :]

        def v_row(i, s):
            return VA[:, s % RA, :] if isinstance(i, int) and i < A_STEPS else VB_[:, s % RB, :]

        def v_row_used(eng, i, s):
            if on_dve(i, s):
                eng.wait_ge(v_added, dve_row(i, s) + 1)
            else:
                eng.wait_ge(v_used, pe_row(i, s) + 1)

        def dg_at(i, s):
            return pe_row(i, s) % RD if isinstance(i, int) else s % RD

        def landed(eng, ina, inb, i, s):
            if isinstance(i, int) and i < A_STEPS:
                eng.wait_ge(ina[s % RA], 16 * (i * (TOPK // RA) + s // RA + 1))
            else:
                eng.wait_ge(inb[s % RB], (i - A_STEPS) * (16 * TOPK // RB) + 16 * (s // RB + 1))

        def load_block(sp, i):
            name, col, _ = BLOCKS[i]
            sp.dma_start(WB[:, i % NW], a[name][0, :, col:col + BW].rearrange("(c p) n -> p c n", p=P)).then_inc(w_in[i % NW], 16)

        block = ctx.enter_context(nc.Block())

        @block.sync
        def _(sp):
            xp = a["x_prompt"].rearrange("b (t p) d -> (b t) p d", p=P)
            sp.dma_start(X[:, 0, :], xp[0]).then_inc(x_in[0], 16)
            load_block(sp, 0)
            for name, r, pat in (("ln_mix_w", SM_MIX, "l (c p) -> (l c) p"), ("mem_norm_w", SM_MEMN, "l (c p) -> (l c) p"),
                                 ("ln_mem_w", SM_LMEM, "l (c p) -> (l c) p"), ("ssd_norm_w", SM_SSD, "l (c p) -> (l c) p"),
                                 ("conv_a_w", SM_CA, "l k (c p) -> (l k c) p"), ("conv_s_w", SM_CS, "l k (c p) -> (l k c) p"),
                                 ("conv_s_b", SM_CB, "l (c p) -> (l c) p"), ("cache_conv_a", SM_HA, "l b k (c p) -> (l b k c) p"),
                                 ("cache_conv_ssd", SM_HS, "l b k (c p) -> (l b k c) p")):
                src = a[name].rearrange(pat, p=P)
                sp.dma_start(SMR[r:r + src.shape[0], :], src).then_inc(small_in, 16)
            sp.dma_start(S0[:, :, :], a["state_ssd"].rearrange("l b (x h) p n -> (h p) (l b x) n", h=2)).then_inc(state_in, 16)
            sp.dma_start(X[:, 1, :], xp[1]).then_inc(x_in[1], 16)
            load_block(sp, 1)
            load_block(sp, 2)
            sp.dma_start(MEM, a["mem_prompt"].rearrange("b (t p) d -> p (b t) d", p=P)).then_inc(mem_in, 16)
            sp.dma_start(WDT[:, :, :], a["w_in"][0, :, 3072:3080].rearrange("(c p) n -> p c n", p=P)).then_inc(wdt_in, 16)
            for i, name in enumerate(("dt_bias", "a_log", "d_skip")):
                sp.dma_start(VB[:, i * HS:(i + 1) * HS], a[name].broadcast_to([P, HS])).then_inc(vec_in, 16)
            for i in range(NW, len(BLOCKS)):
                name, col, key = BLOCKS[i]
                if i == BLOCK_AT[("w_in", 1536, 0)]:
                    for t in range(2, NP):
                        sp.dma_start(X[:, t, :], xp[t]).then_inc(x_in[t], 16)
                    sp.dma_start(X[0:SAM, NP, :], a["x_sample"].rearrange("b p d -> (b p) d")).then_inc(x_in[NP], 16)
                    sp.dma_start(G_FFN[:, :], a["ln_ffn_w"].broadcast_to([P, D])).then_inc(gain_in, 16)
                    sp.dma_start(G_FIN[:, :], a["final_norm_w"].rearrange("(o d) -> o d", o=1).broadcast_to([P, D])).then_inc(gain_in, 16)
                if i == BLOCK_AT[("w_mq", 2 * BW, 0)]:
                    wait_drained(sp, ("kv", 0, 3, 1))
                    sp.dma_start(o["mk"].rearrange("l b (t p) h d -> p (l b t) (h d)", p=P), K0).then_inc(outs, 16)
                    wait_drained(sp, ("kv", 1, 3, 1))
                    sp.dma_start(o["mv"].rearrange("l b (t p) h d -> p (l b t) (h d)", p=P), V0).then_inc(outs, 16)
                if i == BLOCK_AT[("w_mq", 2 * BW, 1)]:
                    wait_drained(sp, ("oc",))
                    for dst, r, k in (("ca_p", 0, 8), ("ca_s", 8, 8), ("cs_p", 16, 24), ("cs_s", 40, 24)):
                        sp.dma_start(o[dst].rearrange("l b k (c p) -> (l b k c) p", p=P), OCT[r:r + k, :]).then_inc(outs, 16)
                    for j, dst in enumerate(("st_p", "st_s")):
                        wait_drained(sp, ("ho", j))
                        sp.dma_start(o[dst].rearrange("l b (x h) p n -> (h p) (l b x) n", h=2),
                                     HO[:, j].rearrange("p (x n) -> p x n", x=4)).then_inc(outs, 16)
                    wait_job(sp, ("o", 1, 3, NP))
                    sp.wait_ge(outs, 16 * 2)
                    sp.dma_start(KB[0], o["mk"].rearrange("l b (t p) h d -> p (l b t) (h d)", p=P)).then_inc(kv_in, 16)
                    sp.dma_start(KB[1], a["cache_mem_k"].rearrange("l b (t p) h d -> p (l b t) (h d)", p=P)).then_inc(kv_in, 16)
                    sp.dma_start(VV[:, 0], o["mv"].rearrange("l b (t p) h d -> p (l b t) (h d)", p=P)).then_inc(kv_in, 16)
                    sp.dma_start(VV[:, 1], a["cache_mem_v"].rearrange("l b (t p) h d -> p (l b t) (h d)", p=P)).then_inc(kv_in, 16)
                for g in range(2):
                    if i == BLOCK_AT[(("w_mo", "w_pq")[g], 0, g)]:
                        if g == 0:
                            wait_job(sp, ("o", 0, 3, 1))
                        else:
                            wait_drained(sp, ("ot", NP, 1))
                        sp.dma_start(SK, a["sub_keys"].rearrange("l h s k d -> k (l h s) d")).then_inc(sk_in, 16)
                wait_job(sp, BLOCKS[i - NW][2])
                load_block(sp, i)
            sp.wait_ge(xs_done, SCALED.index(("norm", 2, NP)) + 1)
            for q in range(1, 4):
                sp.dma_start(XN[q * SAM:(q + 1) * SAM, NP, :], XN[0:SAM, NP, :]).then_inc(relaid_x, 16)
            yp = o["y_prompt"].rearrange("b (t p) d -> (b t) p d", p=P)

            def leave(t):
                sp.wait_ge(y_norm, t + 1)
                dst = yp[t] if t < NP else o["y_sample"].rearrange("b p d -> (b p) d")
                sp.dma_start(dst, XN[0:rows(t), t, :]).then_inc(y_out, 16)

            for t in range(3):
                leave(t)
            sp.wait_ge(topk_s_done, PH)
            for q in range(1, 4):
                sp.dma_start(IDX[q * SAM:(q + 1) * SAM, NP * P:NP * P + 32],
                             IDX[0:SAM, NP * P + 32 * q:NP * P + 32 * q + 32]).then_inc(relaid_i, 16)
            sp.wait_ge(gates_done, 1)
            for q in range(1, 4):
                sp.dma_start(LGF[q * SAM:(q + 1) * SAM, 0:32], LGF[0:SAM, 32 * q:32 * q + 32]).then_inc(relaid_g, 16)
            for t in range(3, NT):
                leave(t)
            sp.wait_ge(y_out, 16 * NT)
            sp.wait_ge(outs, 16 * 8)

        @block.gpsimd
        def _(pool):
            n = [0]

            def link(ins):
                n[0] += 1
                ins.then_inc(const_step, 1)
                pool.wait_ge(const_step, n[0])

            link(pool.memset(ident[:, :], 0.0))
            link(pool.affine_select(out=ident[:, :], in_=ident[:, :], compare_op=ALU.not_equal, fill=1.0, base=0,
                                    pattern=[[-1, P]], channel_multiplier=1))
            link(pool.memset(EPSC[:, :], EPS))
            link(pool.memset(SS[:, :], 1.0))
            pool.memset(tri[:, :], 1.0).then_inc(const_ok, 1)
            pool.wait_ge(const_ok, 1)
            link(pool.affine_select(out=tri[:, :], in_=tri[:, :], compare_op=ALU.is_ge, fill=0.0, base=0,
                                    pattern=[[1, P]], channel_multiplier=-1))
            link(pool.memset(stk[:, :], 0.0))
            for q in range(4):
                link(pool.affine_select(out=stk[:, 0:SAM], in_=stk[:, 0:SAM], compare_op=ALU.not_equal, fill=1.0,
                                        base=-SAM * q, pattern=[[-1, SAM]], channel_multiplier=1))
            link(pool.iota(iota_i[:, :], pattern=[[1, TOPK]], base=0, channel_multiplier=0))
            link(pool.tensor_copy(iota[:, :], iota_i[:, :]))
            link(pool.memset(HU[:, :, :], 0.0))
            link(pool.memset(HX[:, :, :], 0.0))
            link(pool.memset(E3[:, :], 0.0))
            pool.memset(DTV[:, :, :], 0.0).then_inc(const_ok, 1)

            utab = a["u_tab"].rearrange("l e d -> (l e) d")
            vtab = a["v_tab"].rearrange("l e d -> (l e) d")

            def fetch(dst, table, idx, arrived):
                pool.indirect_dma_start(out=dst, out_offset=None, in_=table,
                                        in_offset=bass.IndirectOffsetOnAxis(ap=idx, axis=0)).then_inc(arrived, 16)

            def take(buf, i, before):
                pool.sem_inc(pool_passed, 1)
                pool.tensor_copy(buf, IDX[:, bass.ds(i * TOPK, TOPK)]).then_inc(idx_copied, 1)
                pool.wait_ge(idx_copied, before + 1)
                pool.sem_inc(pool_passed, 1)

            def first_group(i):
                return isinstance(i, int) and i < A_STEPS

            def fetch_u(i, par, s):
                r = RA if first_group(i) else RB
                if not (isinstance(i, int) and (i == 0 or i == A_STEPS) and s < r):
                    pool.wait_ge(u_used, i * TOPK + (s - r + 1))
                    pool.sem_inc(pool_passed, 1)
                fetch(u_row(i, s), utab, IU[:, par, s:s + 1], (ua_in if first_group(i) else ub_in)[s % r])

            def fetch_v(i, par, s):
                r = RA if first_group(i) else RB
                if isinstance(i, int) and i == A_STEPS and s < RB:
                    if s < RA:
                        pool.wait_ge(u_used, A_STEPS * TOPK)
                    else:
                        v_row_used(pool, A_STEPS - 1, TOPK + s - RB)
                    pool.sem_inc(pool_passed, 1)
                elif first_group(i):
                    if i or s >= RA:
                        v_row_used(pool, *((i, s - RA) if s >= RA else (i - 1, TOPK + s - RA)))
                        pool.sem_inc(pool_passed, 1)
                else:
                    pool.wait_ge(v_used, pe_row(i, s) + (1 - RB))
                    pool.sem_inc(pool_passed, 1)
                fetch(v_row(i, s), vtab, IV[:, par, s:s + 1], (va_in if first_group(i) else vb_in)[s % r])

            def step(i, par, with_u=True):
                if with_u:
                    if isinstance(i, int) and i >= NP * PH - 1:
                        pool.wait_ge(relaid_i, 48)
                    else:
                        pool.wait_ge(topk_done, i + 2)
                    take(IU[:, 1 - par, :], i + 1, 1 + 2 * i)
                take(IV[:, par, :], i, (2 + 2 * i) if with_u else (1 + 2 * i))
                for s in range(TOPK):
                    if with_u:
                        fetch_u(i + 1, 1 - par, s)
                    fetch_v(i, par, s)

            pool.wait_ge(outs, 16 * 2)
            pool.wait_ge(topk_done, 1)
            take(IU[:, 0, :], 0, 0)
            for s in range(TOPK):
                fetch_u(0, 0, s)
            for i in range(0, A_STEPS + 2):
                step(i, i % 2)
            with pool.Fori(A_STEPS // 2 + 1, NP * PH // 2 - 1) as j:
                step(2 * j, 0)
                step(2 * j + 1, 1)
            for i in range(NP * PH - 2, STEPS):
                step(i, i % 2, with_u=i + 1 < STEPS)

        @block.tensor
        def _(pe):
            def open_job(key):
                n = SEQN[key]
                if n >= NB:
                    wait_drained(pe, JOBS[n - NB][0])
                return bank_of(key)

            def done(ins):
                ins.then_inc(pe_done, 1)

            def use_block(name, col, g):
                i = BLOCK_AT[(name, col, g)]
                pe.wait_ge(w_in[i % NW], 16 * (i // NW + 1))
                return WB[:, i % NW]

            def transposes(key, parts, n=P):
                b = open_job(key)
                for c, src in enumerate(parts):
                    k = src.shape[0]
                    last = pe.transpose(b[0:n, c * P:c * P + k], src, ident[0:k, 0:k])
                done(last)

            def feature_major(key, w, half, src, n):
                b = open_job(key)
                for c in range(DC):
                    last = pe.matmul(b[:, 0:n], w[:, c, half * P:(half + 1) * P], src[:, c, :], start=(c == 0), stop=(c == DC - 1))
                done(last)

            def token_major(key, w, n, lhs):
                b = open_job(key)
                for c in range(DC):
                    last = pe.matmul(b[0:n, 0:BW], lhs(c), w[:, c, :], start=(c == 0), stop=(c == DC - 1))
                done(last)

            def turn(ph, t):
                pe.wait_ge(xs_done, SCALED.index(("norm", ph, t)) + 1)
                for q in range(2):
                    transposes(("xt", ph, t, q), [XN[0:rows(t), t, (4 * q + c) * P:(4 * q + c + 1) * P] for c in range(4)])

            def const():
                pe.wait_ge(const_ok, 1)
                pe.wait_ge(small_in, 16 * 9)
                transposes("sm", [SMR[:, :]])
                pe.wait_ge(state_in, 16)
                transposes("hi", [S0[:, x, :] for x in range(4)])

            def memn(t):
                pe.wait_ge(xs_done, SCALED.index(("memn", t)) + 1)
                for q in range(2):
                    transposes(("mt", t, q), [MEM[:, t, (4 * q + c) * P:(4 * q + c + 1) * P] for c in range(4)])

            def in_(g, b, m):
                if b == "gc" and m == 0:
                    wait_drained(pe, ("xt", 0, TG[g][-1], 1))
                col = {"gc": 512, "v": 1024, "gb": 0, "x0": 2048, "x1": 2560}[b]
                w = use_block("w_in", col + BW * (m // 2), g)
                feature_major(("in", g, b, m), w, m % 2, XTg[g], NG[g])

            def dt(g):
                b = open_job(("dt", g))
                pe.wait_ge(wdt_in, 16)
                for i, t in enumerate(TG[g]):
                    for c in range(DC):
                        last = pe.matmul(b[0:rows(t), i * HS:(i + 1) * HS], XTg[g][:, c, loc(t)], WDT[:, c, :],
                                         start=(c == 0), stop=(c == DC - 1))
                done(last)

            def z(g, q, t):
                token_major(("z", g, q, t), use_block("w_in", 1536 + BW * q, g), rows(t), lambda c: XTg[g][:, c, loc(t)])

            def oc():
                pe.wait_ge(oc_done, 1)
                transposes(("oc",), [OC[:, :]], 64)

            def kv(k, q, mt):
                token_major(("kv", k, q, mt), use_block(("w_mk", "w_mv")[k], BW * q, 0), P, lambda c: MT[:, c, mt * P:(mt + 1) * P])

            def kt(g, st, q):
                if q == 0:
                    if g == 0:
                        wait_drained(pe, ("kv", 0, 3, 1))
                    else:
                        pe.wait_ge(kv_in, 16 * 4)
                src = K0 if g == 0 else KB[st]
                transposes(("kt", g, st, q), [src[:, mc, (2 * q + j) * P:(2 * q + j + 1) * P] for j in range(2) for mc in range(2)])

            def s1(t):
                if t == TG[group(t)][0]:
                    pe.wait_ge(silu_done, 8 * (group(t) + 1))
                    pe.wait_ge(dta_done, group(t) + 1)
                n, g = rows(t), group(t)
                cs, lt = loc(t, 3), t - TG[g][0]
                b = open_job(("tx", t))
                for c in range(4):
                    last = pe.transpose(b[0:n, c * P:(c + 1) * P], XB[:, c, cs], ident[:, :])
                done(last)
                b = open_job(("tb", t))
                for k in range(2):
                    last = pe.transpose(b[0:n, k * P:(k + 1) * P], XB[:, 4 + k, cs], ident[:, :])
                done(last)
                b = open_job(("ac", t))
                done(pe.matmul(b[0:n, 0:HS], tri[0:n, 0:n], DTV[0:n, 7, lt * HS:(lt + 1) * HS], start=True, stop=True))
                b = open_job(("cb", t))
                for k in range(2):
                    last = pe.matmul(b[0:n, k * P:k * P + n], XB[:, 4 + k, cs], XB[:, 6 + k, cs], start=True, stop=True)
                done(last)

            def s2(t):
                n = rows(t)
                pe.wait_ge(da_done, t + 1)
                for k in range(2):
                    b = open_job(("ab", t, k))
                    for h in range(4):
                        last = pe.matmul(b[:, h * P:h * P + n], DA[0:n, 4 * k + h, :], tri[0:n, 0:n], start=True, stop=True)
                    done(last)

            def s3(t):
                n, st, cs = rows(t), int(t == NP), loc(t, 3)
                b = open_job(("yo", t))
                if st:
                    wait_drained(pe, "hi")
                elif t == 0:
                    pe.wait_ge(h_done, 1)
                else:
                    wait_drained(pe, ("st", t - 1))
                for k in range(2):
                    last = pe.matmul(b[0:n, k * 256:(k + 1) * 256], XB[:, 6 + k, cs], HST[:, st, k * 256:(k + 1) * 256],
                                     start=True, stop=True)
                done(last)
                b = open_job(("yd", t))
                pe.wait_ge(m_done, t + 1)
                pe.wait_ge(xdt_done, t + 1)
                for h in range(HS):
                    last = pe.matmul(b[0:n, h * HP:(h + 1) * HP], LE[0:n, h, 0:n], XDT[0:n, h, :], start=True, stop=True)
                done(last)
                b = open_job(("st", t))
                pe.wait_ge(xdd_done, t + 1)
                wait_drained(pe, ("tb", t))
                for k in range(2):
                    last = pe.matmul(b[:, k * 256:(k + 1) * 256], BT[0:n, k * P:(k + 1) * P],
                                     XDD[0:n, 4 * k:4 * k + 4, :], start=True, stop=True)
                done(last)

            def s4(t):
                pe.wait_ge(xs_done, SCALED.index(("s4", t)) + 1)
                transposes(("yt", t), [Y[0:rows(t), 2 * c:2 * c + 2, :] for c in range(4)])

            def ho(k):
                wait_drained(pe, ("st", NP - 1 + k))
                transposes(("ho", k), [HST[:, k, x * P:(x + 1) * P] for x in range(4)])

            def o_(g, q, t):
                if q == 0:
                    wait_drained(pe, ("yt", t))
                    pe.wait_ge(ya_done, 4 * (g + 1))
                token_major(("o", g, q, t), use_block("w_out", BW * q, g), rows(t),
                            lambda c: GB[:, c, loc(t, 2)] if c < 4 else YBT[:, c - 4, loc(t)])

            def q_(g, m):
                if m == 0:
                    wait_drained(pe, ("xt", 1, TG[g][-1], 1))
                feature_major(("q", g, m), use_block("w_mq", BW * (m // 2), g), m % 2, XTg[g], NG[g])

            def a1(t):
                g, n, st = group(t), rows(t), int(t == NP)
                if t == TG[g][0]:
                    wait_drained(pe, ("q", g, 7))
                    wait_drained(pe, ("kt", g, g, 3))
                kt_ = KT0 if g == 0 else KTB[:, st]
                for hp in range(2):
                    b = open_job(("s", t, hp))
                    for h in range(2):
                        for j in range(2):
                            c = 2 * (2 * hp + h) + j
                            last = pe.matmul(b[0:n, h * NMEM:(h + 1) * NMEM], QTg[g][:, c, loc(t)], kt_[:, c, :],
                                             start=(j == 0), stop=(j == 1))
                    done(last)

            def a2(t):
                g, n, st = group(t), rows(t), int(t == NP)
                v = V0 if g == 0 else VV[:, st]
                pe.wait_ge(p_done, t + 1)
                for q in range(2):
                    transposes(("pt", t, q), [PR[0:n, 2 * q + h, mc * P:(mc + 1) * P] for h in range(2) for mc in range(2)])
                wait_drained(pe, ("pt", t, 1))
                if g == 0:
                    wait_drained(pe, ("kv", 1, 3, 1))
                for q in range(2):
                    b = open_job(("ot", t, q))
                    for c in range(4):
                        h = (4 * q + c) // 2
                        for mc in range(2):
                            last = pe.matmul(b[:, c * P:c * P + n], v[:, mc, (4 * q + c) * P:(4 * q + c + 1) * P],
                                             PT[:, 2 * h + mc, 0:n], start=(mc == 0), stop=(mc == 1))
                    done(last)

            def mo(g, q, t):
                if q == 0:
                    wait_drained(pe, ("ot", t, 1))
                token_major(("mo", g, q, t), use_block("w_mo", BW * q, g), rows(t), lambda c: QTg[g][:, c, loc(t)])

            def sk(g, q):
                pe.wait_ge(sk_in, 16 * (g + 1))
                transposes(("sk", g, q), [SK[:, 4 * q + j, :] for j in range(4)])

            def pq(g, m):
                if m == 0:
                    wait_drained(pe, ("xt", 2, TG[g][-1], 1))
                feature_major(("pq", g, m), use_block("w_pq", BW * (m // 2), g), m % 2, XTg[g], NG[g])

            def sc(t, b4):
                g, n = group(t), rows(t)
                if b4 == 0:
                    wait_drained(pe, ("sk", g, 3))
                wait_drained(pe, ("pq", g, 4 * b4 + 3))
                b = open_job(("sc", t, b4))
                for j in range(4):
                    last = pe.matmul(b[0:n, j * P:(j + 1) * P], QPg[g][:, 4 * b4 + j, loc(t)], SKT[:, 4 * b4 + j, :],
                                     start=True, stop=True)
                done(last)

            def residual_rows(t, **kw):
                n = rows(t)
                for hf in range(2):
                    last = pe.matmul(PSB[:, hf, :], ident[0:n, :], X[0:n, t, hf * 512:(hf + 1) * 512], skip_group_check=True, **kw)
                return last

            def open_tile(t):
                pe.wait_ge(tile_out, t)
                residual_rows(t, start=True, stop=False)

            def close_tile(t):
                pe.wait_ge(v_added, min((t + 1) * PH, SHARED) * QP4 * VE)
                residual_rows(t, start=False, stop=True).then_inc(tile_closed, 1)

            def combine(i, s0=0, s1_=TOPK, close=False):
                for s in range(s0, s1_):
                    if on_dve(i, s):
                        continue
                    landed(pe, va_in, vb_in, i, s)
                    pe.wait_ge(diag_done, pe_row(i, s) + 1)
                    opens = isinstance(i, int) and i < A_STEPS and i % PH == 0 and s == 0
                    if opens and i:
                        pe.wait_ge(tile_out, i // PH)
                    for hf in range(2):
                        last = pe.matmul(PSB[:, hf, :], DG[:, dg_at(i, s), :], v_row(i, s)[:, hf * 512:(hf + 1) * 512],
                                         start=opens, stop=close and s == TOPK - 1, skip_group_check=True)
                    last.then_inc(v_used, 1)

            def quarter(i, k):
                if i >= 1:
                    combine(i - 1, QP4 * k, QP4 * (k + 1))

            does = {"const": const, "turn": turn, "memn": memn, "in": in_, "dt": dt, "z": z, "oc": oc, "kv": kv, "kt": kt,
                    "s1": s1, "s2": s2, "s3": s3, "s4": s4, "ho": ho, "o": o_, "q": q_, "a1": a1, "a2": a2, "mo": mo,
                    "sk": sk, "pq": pq, "sc": sc, "g": quarter, "leave": close_tile}
            for seg in DENSE0 + MIX:
                if seg[0] in does:
                    does[seg[0]](*seg[1:])
            combine(A_STEPS - 1)
            close_tile(1)
            for t in range(2, NP):
                open_tile(t)
                with pe.Fori(t * PH // 2, (t + 1) * PH // 2) as j:
                    combine(2 * j)
                    combine(2 * j + 1)
            open_tile(NP)
            combine(STEPS - 2)
            combine(STEPS - 1, close=True)

        @block.scalar
        def _(act):
            def begin(key):
                wait_job(act, key)
                return bank_of(key)

            def drained(ins):
                ins.then_inc(ev["A"], 1)

            nstep = [0]

            def link(ins):
                nstep[0] += 1
                ins.then_inc(act_step, 1)
                act.wait_ge(act_step, nstep[0])

            def root_mean_square(key, junk, x, n, width):
                col = ROOTS.index(key)
                link(act.activation(junk, x, ACT.Square, scale=width ** -0.5, accum_out=SS[0:n, col:col + 1]))
                act.activation(SS[0:n, col:col + 1], SS[0:n, col:col + 1], ACT.Sqrt, bias=EPSC[0:n, :]).then_inc(root_done, 1)

            def norm(ph, t):
                n, g = rows(t), group(t)
                if ph == 0:
                    act.wait_ge(x_in[t], 16)
                else:
                    wait_drained(act, (("o", "mo")[ph - 1], g, 3, t))
                root_mean_square(("norm", ph, t), XN[0:n, t, :], X[0:n, t, :], n, D)

            def turn(ph, t):
                n, g = rows(t), group(t)
                if ph == 2:
                    for q in range(2):
                        b = begin(("xt", 2, t, q)).rearrange("p (c m) -> p c m", c=4)
                        drained(act.copy(XTg[g][:, 4 * q:4 * q + 4, loc(t)], b[:, :, 0:n]))

            def memn(t):
                act.wait_ge(mem_in, 16)
                wait_job(act, "hi")
                root_mean_square(("memn", t), K0[:, 1, :], MEM[:, t, :], P, D)

            def in_(g, b, m):
                if OWNER[("in", g, b, m)] == "D":
                    return
                dst, base, hist = {"gc": (U, 0, 2), "gb": (GB, 0, 0), "x0": (XB, 0, 3), "x1": (XB, 4, 3)}[b]
                ps = begin(("in", g, b, m))
                for s_, d_ in segs(g, hist):
                    last = act.copy(dst[:, base + m, d_], ps[:, s_])
                drained(last)

            def dt(g):
                w = HS * len(TG[g])
                act.wait_ge(sp_nx, g + 1)
                act.activation(DTV[:, 2, 0:w], DTV[:, 1, 0:w], ACT.Exp).then_inc(sp_e, 1)
                if g == 0:
                    act.wait_ge(vec_in, 48)
                    act.activation(EA[:, :], VB[:, HS:2 * HS], ACT.Exp).then_inc(ea_done, 1)
                act.wait_ge(sp_u, g + 1)
                act.activation(DTV[:, 4, 0:w], DTV[:, 3, 0:w], ACT.Ln).then_inc(sp_l, 1)

            def cs(g, c):
                ln = LX[g] - 3
                act.wait_ge(conv_done, 8 * g + c + 1)
                act.activation(XB[:, c, 0:ln], CT[:, c % 2, 0:ln], ACT.Silu, bias=SMT[:, SM_CB + c:SM_CB + c + 1]).then_inc(silu_done, 1)

            def z(g, q, t):
                b = begin(("z", g, q, t))
                drained(act.activation(ZS[0:rows(t), t - TG[g][0], q * BW:(q + 1) * BW], b[0:rows(t), 0:BW], ACT.Silu))

            def kv(k, q, mt):
                b = begin(("kv", k, q, mt))
                drained(act.copy((K0, V0)[k][:, mt, q * BW:(q + 1) * BW], b[:, 0:BW]))

            def s1(t):
                n = rows(t)
                if t:
                    act.wait_ge(y_done, t)
                b = begin(("tx", t))
                drained(act.copy(XTK[0:n], b[0:n, :].rearrange("p (h q) -> p h q", h=HS)))
                b = begin(("tb", t))
                drained(act.copy(BT[0:n, :], b[0:n, 0:256]))

            def s2(t):
                n = rows(t)
                wait_drained(act, ("ac", t))
                for k in range(2):
                    b = begin(("ab", t, k)).rearrange("p (h l) -> p h l", h=4)
                    act.copy(E3[:, HS + 4 * k:HS + 4 * k + 4], b[:, :, n - 1])
                    for h in range(4):
                        hh = 4 * k + h
                        last = act.activation(LE[0:n, hh, 0:n], b[0:n, h, 0:n], ACT.Relu, bias=E3[0:n, hh:hh + 1], scale=-1.0)
                    drained(last)
                act.wait_ge(ev["A"], ORD[("ab", t, 1)] + 1)
                act.activation(LE[0:n, :, 0:n], LE[0:n, :, 0:n], ACT.Exp, scale=-1.0).then_inc(le_done, 1)
                act.wait_ge(dec_done, t + 1)
                act.activation(EX[:, :], E3[:, :], ACT.Exp).then_inc(ex_done, 1)

            def s4(t):
                n = rows(t)
                act.wait_ge(y_done, t + 1)
                root_mean_square(("s4", t), T1[0:n], Y[0:n], n, DSSD)

            def ho(k):
                drained(act.copy(HO[:, k, :], begin(("ho", k))))

            def kt(g, st, q):
                if g == 1:
                    if st == 0 and q == 0:
                        act.wait_ge(outs, 16 * 8)
                    b = begin(("kt", g, st, q)).rearrange("p (c m) -> p c m", c=2)
                    drained(act.copy(KTB[:, st, 2 * q:2 * q + 2, :], b))

            def q_(g, m):
                if g == 1 and m == 0:
                    wait_job(act, ("kt", 1, 1, 3))
                drained(act.copy(QTg[g][:, m, :], begin(("q", g, m))[:, 0:NG[g]]))

            def a1(t):
                n, o4 = rows(t), (t % 2) * MH
                if t != TG[group(t)][0]:
                    wait_job(act, ("pt", t - 1, 1))
                for hp in range(2):
                    act.wait_ge(mx_done, 2 * t + hp + 1)
                    b = begin(("s", t, hp))
                    for h in range(2):
                        hh = 2 * hp + h
                        last = act.activation(PR[0:n, hh, :], b[0:n, h * NMEM:(h + 1) * NMEM], ACT.Exp,
                                              bias=MX[0:n, o4 + hh:o4 + hh + 1], scale=MD ** -0.5,
                                              accum_out=PSM[0:n, o4 + hh:o4 + hh + 1])
                    drained(last)

            def a2(t):
                g, n = group(t), rows(t)
                for q in range(2):
                    b = begin(("pt", t, q)).rearrange("p (c m) -> p c m", c=4)
                    drained(act.copy(PT[:, 4 * q:4 * q + 4, 0:n], b[:, :, 0:n]))
                for q in range(2):
                    b = begin(("ot", t, q)).rearrange("p (c m) -> p c m", c=4)
                    drained(act.copy(QTg[g][:, 4 * q:4 * q + 4, loc(t)], b[:, :, 0:n]))

            def sk(g, q):
                b = begin(("sk", g, q))
                drained(act.copy(SKT[:, 4 * q:4 * q + 4, :], b.rearrange("p (c m) -> p c m", c=4)))

            def pq(g, m):
                drained(act.copy(QPg[g][:, m, :], begin(("pq", g, m))[:, 0:NG[g]]))

            def sc(t, b4):
                if t == NP and b4 == 0:
                    act.wait_ge(sc_clear, 1)
                dst = SCA[:, t] if t < 2 else SCB[:, t - 2]
                b = begin(("sc", t, b4))
                drained(act.copy(dst[0:rows(t), b4 * 512:(b4 + 1) * 512], b[0:rows(t), :]))

            def gate_exp(i, par):
                act.wait_ge(lg_done, i + 1)
                act.activation(GE[:, par, :], GE[:, par, :], ACT.Exp, accum_out=GSUM[:, par:par + 1]).then_inc(exp_done, 1)

            def gelu(i, par):
                act.wait_ge(u_used, i * TOPK + TOPK)
                act.activation(GH[:, par, :], HID[:, par, :], ACT.Gelu).then_inc(gelu_done, 1)

            def diags(i, par, mat, s0=0, s1_=TOPK):
                if s0 == 0:
                    act.wait_ge(w_done, i + 1)
                for s in range(s0, s1_):
                    if on_dve(i, s):
                        continue
                    if not (isinstance(i, int) and pe_row(i, s) < RD):
                        act.wait_ge(v_used, pe_row(i, s) + (1 - RD))
                    act.activation(DG[:, dg_at(i, s), :], mat, ACT.Copy, scale=WT[:, par, s:s + 1]).then_inc(diag_done, 1)

            def leave(t):
                n = rows(t)
                if t < 2:
                    act.wait_ge(tile_closed, t + 1)
                else:
                    act.wait_ge(v_used, pe_row((t + 1) * PH if t < NP else STEPS, 0))
                for hf in range(2):
                    last = act.copy(X[0:n, t, hf * 512:(hf + 1) * 512], PSB[0:n, hf, :])
                last.then_inc(tile_out, 1)
                act.wait_ge(tile_out, t + 1)
                root_mean_square(("leave", t), XN[0:n, t, :], X[0:n, t, :], n, D)

            def quarter(i, k):
                if i == 0 and k in (1, 2):
                    gate_exp(k - 1, k - 1)
                if i >= 1:
                    diags(i - 1, (i - 1) % 2, ident[:, :], QP4 * k, QP4 * (k + 1))
                    if k == 2:
                        gate_exp(i + 1, (i + 1) % 2)

            def rest(i):
                gelu(i, i % 2)

            act.wait_ge(const_ok, 1)
            does = {"norm": norm, "turn": turn, "memn": memn, "in": in_, "dt": dt, "cs": cs, "z": z, "kv": kv, "s1": s1, "s2": s2, "s4": s4,
                    "ho": ho, "kt": kt, "q": q_, "a1": a1, "a2": a2, "sk": sk, "pq": pq, "sc": sc,
                    "g": quarter, "r": rest, "leave": leave}
            for seg in DENSE0 + MIX:
                if seg[0] in does:
                    does[seg[0]](*seg[1:])
            gate_exp(A_STEPS + 1, 1)
            diags(A_STEPS - 1, 1, ident[:, :])
            leave(1)
            for t in range(2, NP):
                with act.Fori(t * PH // 2, (t + 1) * PH // 2 - (t == NP - 1)) as j:
                    for par in range(2):
                        gelu(2 * j + par, par)
                        gate_exp(2 * j + par + 2, par)
                        diags(2 * j + par, par, ident[:, :])
                if t < NP - 1:
                    leave(t)
            i = NP * PH - 2
            gelu(i, 0)
            diags(i, 0, ident[:, :])
            act.wait_ge(lgs_done, PH)
            act.activation(LGS, LGS, ACT.Exp).then_inc(exps_done, 1)
            gelu(i + 1, 1)
            diags(i + 1, 1, ident[:, :])
            leave(NP - 1)
            for par in range(2):
                gelu(i + 2 + par, par)
                diags(i + 2 + par, par, stk[:, :])
            leave(NP)

        @block.vector
        def _(dve):
            def begin(key):
                wait_job(dve, key)
                return bank_of(key)

            def drained(ins):
                ins.then_inc(ev["D"], 1)

            nstep = [0]

            def link(ins):
                nstep[0] += 1
                ins.then_inc(dve_step, 1)
                dve.wait_ge(dve_step, nstep[0])

            def inv_rms(key, n):
                col = ROOTS.index(key)
                dve.wait_ge(root_done, col + 1)
                link(dve.reciprocal(RS[0:n, col:col + 1], SS[0:n, col:col + 1]))
                return RS[0:n, col:col + 1]

            def scaled_drain(key, dst, col, n):
                b = begin(key).rearrange("p (c m) -> p c m", c=4)[:, :, 0:n]
                drained(dve.tensor_tensor(dst, b, bc(SMT[:, col:col + 4].unsqueeze(2), [P, 4, n]), ALU.mult))

            def const():
                b = begin("sm")
                drained(dve.tensor_copy(SMT[:, :], b[:, 0:SM_ROWS]))
                dve.wait_ge(ev["D"], 1)
                b = begin("hi")
                drained(dve.tensor_copy(HST[:, 1, :], b))
                dve.memset(HST[:, 0, :], 0.0).then_inc(h_done, 1)

            def norm(ph, t):
                n, g = rows(t), group(t)
                rs = inv_rms(("norm", ph, t), n)
                if ph == 2:
                    dve.wait_ge(gain_in, 32)
                    dve.scalar_tensor_tensor(out=XN[0:n, t, :], in0=X[0:n, t, :], scalar=rs, in1=G_FFN[0:n, :],
                                             op0=ALU.mult, op1=ALU.mult).then_inc(xs_done, 1)
                    return
                dve.tensor_scalar(XN[0:n, t, :], X[0:n, t, :], rs, None, ALU.mult).then_inc(xs_done, 1)

            def turn(ph, t):
                n, g = rows(t), group(t)
                for q in range(2 * (ph < 2)):
                    scaled_drain(("xt", ph, t, q), XTg[g][:, 4 * q:4 * q + 4, loc(t)], (SM_MIX, SM_LMEM)[ph] + 4 * q, n)

            def memn(t):
                rs = inv_rms(("memn", t), P)
                dve.tensor_scalar(MEM[:, t, :], MEM[:, t, :], rs, None, ALU.mult).then_inc(xs_done, 1)
                for q in range(2):
                    scaled_drain(("mt", t, q), MT[:, 4 * q:4 * q + 4, t * P:(t + 1) * P], SM_MEMN + 4 * q, P)

            def in_(g, b, m):
                if b == "gc" and m == 0:
                    dve.wait_ge(const_ok, 2)
                    if g == 1:
                        dve.wait_ge(kept, 3)
                        wait_job(dve, ("sc", 1, 3))
                    dve.tensor_copy(U[:, :, 0:2], HU[:, :, :])
                    last = dve.tensor_copy(XB[:, :, 0:3], HX[:, :, :])
                    if g == 1:
                        dve.tensor_copy(U[:, :, 258:260], SMT[:, SM_HA:SM_HA + 8].rearrange("p (k c) -> p c k", k=2))
                        dve.tensor_copy(XB[:, :, 259:262], SMT[:, SM_HS:SM_HS + 24].rearrange("p (k c) -> p c k", k=3))
                        last = dve.memset(GB[:, :, 256:258], 0.0)
                    link(last)
                if OWNER[("in", g, b, m)] == "A":
                    return
                if b == "v":
                    wait_drained(dve, ("in", g, "gc", m))
                    ps = begin(("in", g, b, m))
                    for s_, d_ in segs(g, 2):
                        last = dve.tensor_tensor(U[:, m, d_], ps[:, s_], U[:, m, d_], ALU.mult)
                    drained(last)
                    return
                ps = begin(("in", g, b, m))
                for s_, d_ in segs(g, 3):
                    last = dve.tensor_copy(XB[:, {"x0": 0, "x1": 4}[b] + m, d_], ps[:, s_])
                drained(last)

            def wait_block(g, b):
                for m in (2, 3):
                    wait_drained(dve, ("in", g, b, m))

            def keep(g, b):
                wait_block(g, {"u": "v"}.get(b, b))
                nk, c0, nc_, src, hist = (2, 0, 4, U, HU) if b == "u" else (3, {"x0": 0, "x1": 4}[b], 4, XB, HX)
                s1_ = slice(c0, c0 + nc_)
                if g == 0:
                    dve.tensor_copy(hist[:, s1_, :], src[:, s1_, 256:256 + nk]).then_inc(kept, 1)
                    return
                width = 4 if b == "u" else 8
                for j, first in ((0 if b == "u" else 16, 256), (8 if b == "u" else 40, 256 + SAM + nk)):
                    dst = OC[:, j:j + nk * width].rearrange("p (k c) -> p c k", k=nk)[:, s1_, :]
                    last = dve.tensor_copy(dst, src[:, s1_, first:first + nk])
                if b == "x1":
                    last.then_inc(oc_done, 1)
                else:
                    link(last)

            def ca(g, c):
                if c == 0:
                    wait_block(g, "gb")
                ln = LG[g]
                w = lambda k: SMT[:, SM_CA + 4 * k + c:SM_CA + 4 * k + c + 1]
                acc = CT[:, c % 2, 0:ln]
                link(dve.tensor_scalar(acc, U[:, c, 0:ln], w(0), None, ALU.mult))
                for k in (1, 2):
                    link(dve.scalar_tensor_tensor(out=acc, in0=U[:, c, k:k + ln], scalar=w(k), in1=acc, op0=ALU.mult, op1=ALU.add))
                dve.tensor_tensor(GB[:, c, 0:ln], GB[:, c, 0:ln], acc, ALU.mult).then_inc(ya_done, 1)
                dve.wait_ge(ya_done, 4 * g + c + 1)

            def cs(g, c):
                ln = LX[g] - 3
                w = lambda k: SMT[:, SM_CS + 8 * k + c:SM_CS + 8 * k + c + 1]
                if c >= 2:
                    dve.wait_ge(silu_done, 8 * g + c - 1)
                wait_drained(dve, ("in", g, "x0" if c < 4 else "x1", c % 4))
                if c == 4 and g == 1:
                    dve.wait_ge(oc_done, 1)
                if c in (0, 4) and g == 0:
                    dve.wait_ge(kept, 2 if c == 0 else 3)
                acc = CT[:, c % 2, 0:ln]
                link(dve.tensor_scalar(acc, XB[:, c, 0:ln], w(0), None, ALU.mult))
                for k in (1, 2):
                    link(dve.scalar_tensor_tensor(out=acc, in0=XB[:, c, k:k + ln], scalar=w(k), in1=acc, op0=ALU.mult, op1=ALU.add))
                dve.scalar_tensor_tensor(out=acc, in0=XB[:, c, 3:3 + ln], scalar=w(3), in1=acc, op0=ALU.mult, op1=ALU.add).then_inc(conv_done, 1)

            def dt(g):
                w, nt = HS * len(TG[g]), len(TG[g])
                r = lambda k: DTV[:, k, 0:w]
                b = begin(("dt", g))
                dve.wait_ge(vec_in, 48)
                dve.wait_ge(const_ok, 2)
                if g == 1:
                    dve.tensor_tensor(DTV[0:SAM, 0, 2 * HS:3 * HS], b[0:SAM, 2 * HS:3 * HS], VB[0:SAM, 0:HS], ALU.add)
                drained(dve.tensor_tensor(DTV[:, 0, 0:2 * HS].rearrange("p (t h) -> p t h", h=HS),
                                          b[:, 0:2 * HS].rearrange("p (t h) -> p t h", h=HS),
                                          bc(VB[:, 0:HS].unsqueeze(1), [P, 2, HS]), ALU.add))
                dve.wait_ge(ev["D"], ORD[("dt", g)] + 1)
                dve.scalar_tensor_tensor(out=r(1), in0=r(0), scalar=-1.0, in1=r(0), op0=ALU.mult, op1=ALU.min).then_inc(sp_nx, 1)
                dve.wait_ge(sp_e, g + 1)
                dve.tensor_scalar(r(3), r(2), 1.0, None, ALU.add).then_inc(sp_u, 1)
                dve.wait_ge(sp_u, g + 1)
                link(dve.tensor_scalar(r(5), r(3), -1.0, None, ALU.add))
                link(dve.scalar_tensor_tensor(out=r(7), in0=r(5), scalar=0.0, in1=r(2), op0=ALU.is_equal, op1=ALU.mult))
                dve.wait_ge(sp_l, g + 1)
                link(dve.scalar_tensor_tensor(out=r(4), in0=r(5), scalar=0.0, in1=r(4), op0=ALU.not_equal, op1=ALU.mult))
                link(dve.tensor_scalar(r(5), r(5), 2.0 ** -24, None, ALU.max))
                link(dve.reciprocal(r(5), r(5)))
                link(dve.tensor_tensor(r(4), r(4), r(2), ALU.mult))
                link(dve.tensor_tensor(r(4), r(4), r(5), ALU.mult))
                link(dve.tensor_tensor(r(4), r(4), r(7), ALU.add))
                link(dve.scalar_tensor_tensor(out=r(6), in0=r(0), scalar=0.0, in1=r(4), op0=ALU.max, op1=ALU.add))
                dve.wait_ge(ea_done, 1)
                v3 = lambda k: r(k).rearrange("p (t h) -> p t h", h=HS)
                dve.scalar_tensor_tensor(out=v3(7), in0=v3(6), scalar=-1.0, in1=bc(EA[:, :].unsqueeze(1), [P, nt, HS]),
                                         op0=ALU.mult, op1=ALU.mult).then_inc(dta_done, 1)
                dve.wait_ge(dta_done, g + 1)

            def oc():
                drained(dve.tensor_copy(OCT[:, :], begin(("oc",))[0:64, 0:P]))

            def kt(g, st, q):
                if g == 0:
                    b = begin(("kt", g, st, q)).rearrange("p (c m) -> p c m", c=2)
                    drained(dve.tensor_copy(KT0[:, 2 * q:2 * q + 2, :], b))

            def s1(t):
                n, g = rows(t), group(t)
                lt = t - TG[g][0]
                dve.tensor_copy(DA[0:n], bc(DTV[0:n, 7, lt * HS:(lt + 1) * HS].unsqueeze(2), [n, HS, P])).then_inc(da_done, 1)
                b = begin(("ac", t))
                drained(dve.tensor_copy(E3[0:n, 0:HS], b[0:n, 0:HS]))
                b = begin(("cb", t)).rearrange("p (g l) -> p g l", g=4)
                drained(dve.tensor_tensor(CBM[0:n, :, 0:n], b[0:n, 0:2, 0:n], bc(tri[0:n, 0:n].unsqueeze(1), [n, 2, n]), ALU.mult))
                wait_drained(dve, ("tx", t))
                dve.tensor_tensor(XDT[0:n], XTK[0:n], bc(DTV[0:n, 6, lt * HS:(lt + 1) * HS].unsqueeze(2), [n, HS, HP]),
                                  ALU.mult).then_inc(xdt_done, 1)

            def s2(t):
                n = rows(t)
                wait_drained(dve, ("ab", t, 1))
                dve.wait_ge(ev["D"], ORD[("cb", t)] + 1)
                dve.tensor_tensor(E3[0:n, 2 * HS:], E3[0:n, HS:2 * HS], E3[0:n, 0:HS], ALU.subtract).then_inc(dec_done, 1)
                dve.wait_ge(le_done, t + 1)
                for k in range(2):
                    last = dve.tensor_tensor(LE[0:n, 4 * k:4 * k + 4, 0:n], LE[0:n, 4 * k:4 * k + 4, 0:n],
                                             bc(CBM[0:n, k:k + 1, 0:n], [n, 4, n]), ALU.mult)
                last.then_inc(m_done, 1)
                dve.wait_ge(ex_done, t + 1)
                dve.wait_ge(xdt_done, t + 1)
                dve.tensor_tensor(XDD[0:n], XDT[0:n], bc(EX[0:n, 2 * HS:].unsqueeze(2), [n, HS, HP]), ALU.mult).then_inc(xdd_done, 1)

            def s3(t):
                n, g, st = rows(t), group(t), int(t == NP)
                lt = t - TG[g][0]
                b = begin(("yo", t)).rearrange("p (h q) -> p h q", h=HS)
                dve.tensor_tensor(T1[0:n], b[0:n], bc(EX[0:n, 0:HS].unsqueeze(2), [n, HS, HP]), ALU.mult).then_inc(ev["D"], 1)
                hst = HST[:, st, :].rearrange("p (h q) -> p h q", h=HS)
                link(dve.tensor_tensor(hst, hst, bc(EX[:, HS:2 * HS].unsqueeze(2), [P, HS, HP]), ALU.mult))
                b = begin(("yd", t)).rearrange("p (h q) -> p h q", h=HS)
                dve.tensor_tensor(T1[0:n], T1[0:n], b[0:n], ALU.add).then_inc(ev["D"], 1)
                if t:
                    wait_job(dve, ("yt", t - 1))
                link(dve.tensor_tensor(Y[0:n], XTK[0:n], bc(VB[0:n, 2 * HS:].unsqueeze(2), [n, HS, HP]), ALU.mult))
                b = begin(("st", t))
                dve.tensor_tensor(HST[:, st, :], HST[:, st, :], b, ALU.add).then_inc(ev["D"], 1)
                link(dve.tensor_tensor(Y[0:n], Y[0:n], T1[0:n], ALU.add))
                dve.tensor_tensor(Y[0:n], Y[0:n], ZS[0:n, lt, :].rearrange("p (h q) -> p h q", h=HS), ALU.mult).then_inc(y_done, 1)

            def s4(t):
                n = rows(t)
                rs = inv_rms(("s4", t), n)
                dve.wait_ge(y_done, t + 1)
                dve.tensor_scalar(Y[0:n], Y[0:n], rs, None, ALU.mult).then_inc(xs_done, 1)
                scaled_drain(("yt", t), YBT[:, :, loc(t)], SM_SSD, n)

            def residual(kind):
                def add(g, q, t):
                    n = rows(t)
                    b = begin((kind, g, q, t))
                    xs = X[0:n, t, q * BW:(q + 1) * BW]
                    drained(dve.tensor_tensor(xs, b[0:n, 0:BW], xs, ALU.add))
                return add

            def a1(t):
                n, o4 = rows(t), (t % 2) * MH
                for hp in range(2):
                    b = begin(("s", t, hp)).rearrange("p (h m) -> p h m", h=2)
                    mx = MX[0:n, o4 + 2 * hp:o4 + 2 * hp + 2]
                    link(dve.tensor_reduce(mx, b[0:n], AXX, ALU.max))
                    dve.tensor_scalar(mx, mx, -MD ** -0.5, None, ALU.mult).then_inc(mx_done, 1)
                wait_drained(dve, ("s", t, 1))
                rc = PSM[0:n, 2 * MH + o4:2 * MH + o4 + MH]
                link(dve.reciprocal(rc, PSM[0:n, o4:o4 + MH]))
                dve.tensor_tensor(PR[0:n], PR[0:n], bc(rc.unsqueeze(2), [n, MH, NMEM]), ALU.mult).then_inc(p_done, 1)

            def sc(t, b4):
                if t == NP and b4 == 0:
                    wait_job(dve, ("pq", 1, 15))
                    wait_job(dve, ("sk", 1, 3))
                    dve.memset(SCB[:, 2, :], 0.0).then_inc(sc_clear, 1)

            def routing(call, src, idx_at, finished):
                base = call * TOPK_LINKS
                k = [0]

                def also(ins):
                    k[0] += 1
                    ins.then_inc(topk_step, 1)

                def sync(plain=False):
                    dve.wait_ge(topk_step, base + k[0])
                    if not plain and not isinstance(base, int):
                        dve.sem_inc(dve_passed, 1)

                def keys():
                    also(dve.tensor_copy(TS[:, :, :].rearrange("p a b -> p (a b)"), src))
                    sync()
                    for h in range(2):
                        also(dve.max(TV[:, h, 0:8], TS[:, h, :]))
                    sync()
                    for h in range(2):
                        also(dve.max_index(TI[:, h, 0:8], TV[:, h, 0:8], TS[:, h, :]))
                        also(dve.match_replace(TS2[:, h, :], TV[:, h, 0:8], TS[:, h, :], NEG))

                def keys2():
                    sync()
                    for h in range(2):
                        also(dve.max(TV[:, h, 8:16], TS2[:, h, :]))
                    sync()
                    for h in range(2):
                        also(dve.max_index(TI[:, h, 8:16], TV[:, h, 8:16], TS2[:, h, :]))
                    also(dve.tensor_tensor(CO, bc(TV[:, 0, :].unsqueeze(2), [P, TOPK, TOPK]), bc(TV[:, 1:2, :], [P, TOPK, TOPK]), ALU.add))
                    sync()
                    also(dve.max(CV[:, 0:8], COF))

                def pairs():
                    sync()
                    also(dve.max_index(CP[:, 0:8], CV[:, 0:8], COF))
                    also(dve.match_replace(CO2, CV[:, 0:8], COF, NEG))
                    sync()
                    also(dve.max(CV[:, 8:16], CO2))
                    sync()
                    also(dve.max_index(CP[:, 8:16], CV[:, 8:16], CO2))
                    sync(plain=True)
                    also(dve.tensor_scalar(CA[:, 0, :], CP, 4, None, ALU.logical_shift_right))
                    also(dve.tensor_scalar(CA[:, 1, :], CP, 15, None, ALU.bitwise_and))

                def experts():
                    e3 = [EQ[:, h, :].rearrange("p (k j) -> p k j", j=TOPK) for h in range(2)]
                    sync(plain=True)
                    for h in range(2):
                        also(dve.tensor_tensor(e3[h], bc(CA[:, h, :].unsqueeze(2), [P, TOPK, TOPK]),
                                               bc(iota[:, :].unsqueeze(1), [P, TOPK, TOPK]), ALU.is_equal))
                    sync(plain=True)
                    for h in range(2):
                        also(dve.tensor_tensor(e3[h], e3[h], bc(TI[:, h:h + 1, :], [P, TOPK, TOPK]), ALU.mult))
                    sync(plain=True)
                    also(dve.tensor_reduce(EQS, EQ.rearrange("p h (k j) -> p h k j", j=TOPK), AXX, ALU.add))
                    sync(plain=True)
                    dve.scalar_tensor_tensor(out=IDX[:, bass.ds(idx_at, TOPK)], in0=EQS[:, 0, :], scalar=float(NK),
                                             in1=EQS[:, 1, :], op0=ALU.mult, op1=ALU.add).then_inc(finished, 1)
                    assert k[0] == TOPK_LINKS, k[0]

                return [keys, keys2, pairs, experts]

            def scores(i):
                if isinstance(i, int) and i < A_STEPS:
                    return SCA.rearrange("p t k -> p (t k)")[:, i * 256:(i + 1) * 256]
                return SCB.rearrange("p t k -> p (t k)")[:, bass.ds((i - A_STEPS) * 256, 256)]

            def route(i, call):
                return routing(call, scores(i), i * TOPK, topk_done)

            def logits(i, par):
                if not (isinstance(i, int) and i < 2):
                    dve.wait_ge(w_done, i - 1)
                dve.tensor_scalar(GE[:, par, :], CV, CV[:, 0:1], None, ALU.subtract).then_inc(lg_done, 1)

            def dots(i, par, x, s0=0, s1_=TOPK):
                for s in range(s0, s1_):
                    landed(dve, ua_in, ub_in, i, s)
                    u = u_row(i, s)
                    dve.tensor_tensor_reduce(u, u, x, 1.0, 0.0, ALU.mult, ALU.add, HID[:, par, s:s + 1]).then_inc(u_used, 1)

            def gated(i, par):
                if isinstance(i, int) and 2 <= i < A_STEPS + 2:
                    dve.wait_ge(v_added, min(i - 1, SHARED) * QP4 * VE)
                dve.wait_ge(exp_done, i + 1)
                dve.reciprocal(GR[:, par:par + 1], GSUM[:, par:par + 1]).then_inc(gr_done, 1)
                dve.wait_ge(gr_done, i + 1)
                dve.wait_ge(gelu_done, i + 1)
                dve.scalar_tensor_tensor(out=WT[:, par, :], in0=GE[:, par, :], scalar=GR[:, par:par + 1], in1=GH[:, par, :],
                                         op0=ALU.mult, op1=ALU.mult).then_inc(w_done, 1)

            def add_rows(i, s0=0, s1_=TOPK):
                for s in range(s0, s1_):
                    if on_dve(i, s):
                        landed(dve, va_in, vb_in, i, s)
                        dve.wait_ge(w_done, i + 1)
                        if dve_row(i, s):
                            dve.wait_ge(v_added, dve_row(i, s))
                        x = X[:, i // PH, :]
                        dve.scalar_tensor_tensor(out=x, in0=v_row(i, s), scalar=WT[:, i % 2, s:s + 1], in1=x, op0=ALU.mult,
                                                 op1=ALU.add).then_inc(v_added, 1)

            def final(t):
                n = rows(t)
                rs = inv_rms(("leave", t), n)
                dve.scalar_tensor_tensor(out=XN[0:n, t, :], in0=X[0:n, t, :], scalar=rs, in1=G_FIN[0:n, :],
                                         op0=ALU.mult, op1=ALU.mult).then_inc(y_norm, 1)

            pieces = {}

            def start():
                wait_drained(dve, ("sc", 0, 0))
                for f in route(0, 0):
                    f()
                dve.wait_ge(topk_done, 1)
                logits(0, 0)

            def quarter(i, k):
                dots(i, i % 2, XN[:, i // PH, :], QP4 * k, QP4 * (k + 1))
                if i == 0:
                    if k % 2 == 0:
                        pieces[0] = route(1 + k // 2, 1 + k // 2)
                        wait_drained(dve, ("sc", 0, k // 2))
                    for f in pieces[0][2 * (k % 2):][:2]:
                        f()
                    if k == 1:
                        dve.wait_ge(topk_done, 2)
                        logits(1, 1)
                    return
                if k == 0:
                    if i + 2 < A_STEPS:
                        wait_drained(dve, ("sc", (i + 2) // PH, (i + 2) % PH // 2))
                    if i + 2 == A_STEPS:
                        for t in TG[1]:
                            wait_drained(dve, ("sc", t, 3))
                    pieces[i] = route(i + 2, i + 2)
                pieces[i][k]()
                if k < 3:
                    add_rows(i - 1, QP4 * k, QP4 * (k + 1))

            def rest(i):
                gated(i, i % 2)
                dve.wait_ge(w_done, i + 1)
                logits(i + 2, i % 2)
                if i >= 1:
                    add_rows(i - 1, 3 * QP4, TOPK)

            does = {"const": const, "norm": norm, "turn": turn, "memn": memn, "in": in_, "keep": keep, "ca": ca, "cs": cs, "dt": dt, "oc": oc,
                    "kt": kt, "s1": s1, "s2": s2, "s3": s3, "s4": s4, "o": residual("o"), "a1": a1, "mo": residual("mo"),
                    "sc": sc, "start": start, "g": quarter, "r": rest, "final": final}
            for seg in DENSE0:
                if seg[0] in does:
                    does[seg[0]](*seg[1:])
            for seg in MIX:
                if seg[0] in does:
                    does[seg[0]](*seg[1:])
            first_call = A_STEPS + 2

            def sample_route(p):
                for f in routing(first_call + 3 * (p - A_STEPS // 2) + 1,
                                 SCB.rearrange("p t k -> p (t k)")[:, bass.ds((p - A_STEPS // 2) * 256 + 2 * 2048, 256)],
                                 (p - A_STEPS // 2) * TOPK + NP * P, topk_s_done):
                    f()
                dve.tensor_scalar(LGF[:, bass.ds((p - A_STEPS // 2) * TOPK, TOPK)], CV, CV[:, 0:1], None, ALU.subtract).then_inc(lgs_done, 1)

            def pair(j, t):
                for par in range(2):
                    i = 2 * j + par
                    dots(i, par, XN[:, t, :])
                    for f in route(i + 2, first_call + 3 * (j - A_STEPS // 2) + 2 * par):
                        f()
                    gated(i, par)
                    logits(i + 2, par)
                    if par == 0:
                        sample_route(j)

            with dve.Fori(A_STEPS // 2, A_STEPS // 2 + PH // 2) as j:
                pair(j, 2)
            final(1)
            with dve.Fori(A_STEPS // 2 + PH // 2, A_STEPS - 1) as j:
                pair(j, 3)
            final(2)
            i = NP * PH - 2
            dots(i, 0, XN[:, 3, :])
            sample_last = A_STEPS - 1
            for f in routing(first_call + 3 * (sample_last - A_STEPS // 2), SCB.rearrange("p t k -> p (t k)")[:, 2 * 2048 + 7 * 256:3 * 2048],
                             7 * TOPK + NP * P, topk_s_done):
                f()
            dve.tensor_scalar(LGF[:, 7 * TOPK:8 * TOPK], CV, CV[:, 0:1], None, ALU.subtract).then_inc(lgs_done, 1)
            gated(i, 0)
            dots(i + 1, 1, XN[:, 3, :])
            gated(i + 1, 1)
            dve.wait_ge(exps_done, 1)
            dve.tensor_reduce(GS[:, 0, :], LGS, AXX, ALU.add).then_inc(gates_step, 1)
            dve.wait_ge(gates_step, 1)
            dve.reciprocal(GS[:, 1, :], GS[:, 0, :]).then_inc(gates_step, 1)
            dve.wait_ge(gates_step, 2)
            dve.tensor_tensor(LGS, LGS, bc(GS[:, 1, :].unsqueeze(2), [P, PH, TOPK]), ALU.mult).then_inc(gates_done, 1)
            dve.wait_ge(relaid_x, 48)
            for par in range(2):
                dots(i + 2 + par, par, XN[:, NP, :])
                dve.wait_ge(relaid_g, 48)
                dve.wait_ge(gates_done, 1)
                dve.wait_ge(gelu_done, i + 3 + par)
                dve.tensor_tensor(WT[:, par, :], LGF[:, par * TOPK:(par + 1) * TOPK], GH[:, par, :], ALU.mult).then_inc(w_done, 1)
            final(3)
            final(4)


_INS = ["x_prompt", "x_sample", "mem_prompt", "cache_conv_a", "cache_conv_ssd", "state_ssd", "cache_mem_k", "cache_mem_v",
        "ln_mix_w", "w_in", "conv_a_w", "conv_s_w", "conv_s_b", "dt_bias", "a_log", "d_skip", "ssd_norm_w", "w_out",
        "ln_mem_w", "mem_norm_w", "w_mq", "w_mk", "w_mv", "w_mo", "ln_ffn_w", "w_pq", "sub_keys", "u_tab", "v_tab",
        "final_norm_w"]
_OUTS = [("y_prompt", (1, 512, 1024)), ("y_sample", (1, 32, 1024)), ("ca_p", (1, 1, 2, 512)), ("cs_p", (1, 1, 3, 1024)),
         ("st_p", (1, 1, 8, 64, 128)), ("mk", (1, 1, 256, 4, 256)), ("mv", (1, 1, 256, 4, 256)),
         ("ca_s", (1, 1, 2, 512)), ("cs_s", (1, 1, 3, 1024)), ("st_s", (1, 1, 8, 64, 128))]


def kernel(**inputs):
    import numpy as _np
    import concourse.bacc as _bacc
    from concourse import mybir as _mybir
    from concourse.bass_utils import run_bass_kernel_spmd as _run

    nc = _bacc.Bacc("TRN2", target_bir_lowering=False, num_devices=1)
    arrays, ins, outs = {}, {}, {}
    for name in _INS:
        arr = _np.ascontiguousarray(inputs[name])
        arrays[f"in_{name}"] = arr
        ins[name] = nc.dram_tensor(f"in_{name}", arr.shape, _mybir.dt.from_np(arr.dtype), kind="ExternalInput").ap()
    for name, shape in _OUTS:
        outs[name] = nc.dram_tensor(f"out_{name}", shape, _mybir.dt.float32, kind="ExternalOutput").ap()
    build_program(nc, ins, outs)
    r = _run(nc, [arrays], core_ids=[0])
    return tuple(r.results[0][f"out_{name}"] for name, _ in _OUTS)
```
